# Optimizing a Trainium2 kernel written in Bass

```python
import math
import jax, jax.numpy as jnp
from jax import lax
import numpy as np

D_MODEL = 2048
BATCH = 1
SEQ = 256
DEPTH = 1

HEAD_DIM = 64
LRU_WIDTH = D_MODEL // 2
LRU_HEADS = LRU_WIDTH // HEAD_DIM
LRU_HEAD_DIM = HEAD_DIM
ATTN_WIDTH = D_MODEL - LRU_WIDTH
ATTN_HEADS = ATTN_WIDTH // HEAD_DIM
ATTN_HEAD_DIM = HEAD_DIM
MIX_WIDTH = LRU_WIDTH + ATTN_WIDTH
IN_PROJ_WIDTH = 2 * LRU_WIDTH + 3 * ATTN_WIDTH
CONV_WIDTH = 4
RG_C = 8.0
GRID_W = 64
WIN_ROWS = 8
WIN_COLS = 16
D_FF = 256 * math.ceil(8 * D_MODEL / 3 / 256)
NORM_EPS = 1e-6

kernel_name = "hybrid_rglru_natten_macaron"

def rms_norm(x, g):
    xf = x.astype(jnp.float32)
    y = xf * lax.rsqrt(jnp.mean(xf * xf, axis=-1, keepdims=True) + NORM_EPS) * g.astype(jnp.float32)
    return y.astype(x.dtype)

def swiglu(u, w_in, w_out):
    gate, up = jnp.split(u @ w_in, 2, axis=-1)
    return (jax.nn.silu(gate) * up) @ w_out

def _lin_rec_combine(left, right):
    a_l, b_l = left
    a_r, b_r = right
    return a_l * a_r, a_r * b_l + b_r

def rglru_mixer(x_in, gate_in, conv_w, conv_b, gate_w, gate_b, lam):
    B, S, C = x_in.shape
    pad_l = CONV_WIDTH // 2
    xc = lax.conv_general_dilated(
        x_in, conv_w[:, None, :], window_strides=(1,),
        padding=[(pad_l, CONV_WIDTH - 1 - pad_l)],
        dimension_numbers=("NWC", "WIO", "NWC"), feature_group_count=C) + conv_b
    xf = xc.astype(jnp.float32)
    xh = xf.reshape(B, S, LRU_HEADS, LRU_HEAD_DIM)
    gates = jax.nn.sigmoid(
        jnp.einsum("bshi,zghij->zgbshj", xh, gate_w.astype(jnp.float32))
        + gate_b.astype(jnp.float32)[:, :, None, None])
    gates = gates.reshape(2, 2, B, S, C)
    r, i = gates[:, 0], gates[:, 1]
    log_a = -RG_C * r * jax.nn.softplus(-lam.astype(jnp.float32))[:, None, None, :]
    a = jnp.exp(log_a)
    b = jnp.sqrt(-jnp.expm1(2.0 * log_a)) * (i * xf)
    h_fwd = lax.associative_scan(_lin_rec_combine, (a[0], b[0]), axis=1)[1]
    h_bwd = lax.associative_scan(_lin_rec_combine, (a[1], b[1]), axis=1, reverse=True)[1]
    y = jax.nn.gelu(gate_in.astype(jnp.float32)) * (h_fwd + h_bwd)
    return y.astype(x_in.dtype)

def neighbourhood_attention(q, k, v, rpb):
    B, S, _ = q.shape
    rows = S // GRID_W
    kr = min(WIN_ROWS, rows)
    grid = (B, rows, GRID_W, ATTN_HEADS, ATTN_HEAD_DIM)
    scale = ATTN_HEAD_DIM ** -0.5
    qg = q.reshape(grid).astype(jnp.float32) * scale
    kg = k.reshape(grid).astype(jnp.float32)
    vg = v.reshape(grid).astype(jnp.float32)
    cols = jnp.arange(GRID_W)
    col_start = jnp.clip(cols - WIN_COLS // 2, 0, GRID_W - WIN_COLS)
    col_idx = col_start[:, None] + jnp.arange(WIN_COLS)
    sel = jax.nn.one_hot(col_idx, GRID_W, dtype=jnp.float32)
    col_bias = rpb.astype(jnp.float32)[:, :, col_idx - cols[:, None] + WIN_COLS - 1]

    def row_block(r):
        rs = jnp.clip(r - kr // 2, 0, rows - kr)
        q_row = lax.dynamic_index_in_dim(qg, r, axis=1, keepdims=False)
        k_band = lax.dynamic_slice_in_dim(kg, rs, kr, axis=1)
        v_band = lax.dynamic_slice_in_dim(vg, rs, kr, axis=1)
        s_band = jnp.einsum("bqhd,brkhd->bhqrk", q_row, k_band)
        s = jnp.einsum("bhqrk,qwk->bhqrw", s_band, sel)
        row_off = rs + jnp.arange(kr) - r + WIN_ROWS - 1
        bias = jnp.take(col_bias, row_off, axis=1).transpose(0, 2, 1, 3)
        s = s + bias[None]
        p = jax.nn.softmax(s.reshape(B, ATTN_HEADS, GRID_W, kr * WIN_COLS), axis=-1)
        p = p.reshape(B, ATTN_HEADS, GRID_W, kr, WIN_COLS)
        p_band = jnp.einsum("bhqrw,qwk->bhqrk", p, sel)
        return jnp.einsum("bhqrk,brkhd->bqhd", p_band, v_band)

    out = lax.map(row_block, jnp.arange(rows))
    return out.transpose(1, 0, 2, 3, 4).reshape(B, S, ATTN_WIDTH).astype(q.dtype)

def setup_inputs(seed: int = 0) -> dict:
    key = jax.random.key(seed)
    ks = jax.random.split(key, 24)
    f32 = jnp.float32
    L = DEPTH

    def nrm(k, shape, scale):
        return jax.random.normal(k, shape, f32) * scale

    def gain(k, shape):
        return 1.0 + 0.05 * jax.random.normal(k, shape, f32)

    a_c = jax.random.uniform(ks[10], (L, 2, LRU_WIDTH), f32, 0.9, 0.999)
    a_base = a_c ** (1.0 / RG_C)
    lru_lambda = jnp.log(a_base) - jnp.log1p(-a_base)
    return {
        "x": nrm(ks[0], (BATCH, SEQ, D_MODEL), 1.0),
        "norm_ffn1": gain(ks[1], (L, D_MODEL)),
        "ffn1_w_in": nrm(ks[2], (L, D_MODEL, 2 * D_FF), D_MODEL ** -0.5),
        "ffn1_w_out": nrm(ks[3], (L, D_FF, D_MODEL), D_FF ** -0.5),
        "norm_mix": gain(ks[4], (L, D_MODEL)),
        "w_in_mix": nrm(ks[5], (L, D_MODEL, IN_PROJ_WIDTH), D_MODEL ** -0.5),
        "lru_conv_w": nrm(ks[6], (L, CONV_WIDTH, LRU_WIDTH), CONV_WIDTH ** -0.5),
        "lru_conv_b": nrm(ks[7], (L, LRU_WIDTH), 0.01),
        "lru_gate_w": nrm(ks[8], (L, 2, 2, LRU_HEADS, LRU_HEAD_DIM, LRU_HEAD_DIM), LRU_HEAD_DIM ** -0.5),
        "lru_gate_b": nrm(ks[9], (L, 2, 2, LRU_HEADS, LRU_HEAD_DIM), 0.01),
        "lru_lambda": lru_lambda,
        "attn_rpb": nrm(ks[11], (L, ATTN_HEADS, 2 * WIN_ROWS - 1, 2 * WIN_COLS - 1), 0.02),
        "lru_out_norm": gain(ks[12], (L, LRU_WIDTH)),
        "attn_out_norm": gain(ks[13], (L, ATTN_WIDTH)),
        "w_out_mix": nrm(ks[14], (L, MIX_WIDTH, D_MODEL), MIX_WIDTH ** -0.5),
        "norm_ffn2": gain(ks[15], (L, D_MODEL)),
        "ffn2_w_in": nrm(ks[16], (L, D_MODEL, 2 * D_FF), D_MODEL ** -0.5),
        "ffn2_w_out": nrm(ks[17], (L, D_FF, D_MODEL), D_FF ** -0.5),
        "norm_final": gain(ks[18], (D_MODEL,)),
    }

def reference(x, norm_ffn1, ffn1_w_in, ffn1_w_out, norm_mix, w_in_mix, lru_conv_w, lru_conv_b,
              lru_gate_w, lru_gate_b, lru_lambda, attn_rpb, lru_out_norm, attn_out_norm,
              w_out_mix, norm_ffn2, ffn2_w_in, ffn2_w_out, norm_final):
    h = x
    for l in range(DEPTH):
        h = h + 0.5 * swiglu(rms_norm(h, norm_ffn1[l]), ffn1_w_in[l], ffn1_w_out[l])
        u = rms_norm(h, norm_mix[l])
        proj = u @ w_in_mix[l]
        x_lru, g_lru, q, k, v = jnp.split(
            proj, [LRU_WIDTH, 2 * LRU_WIDTH, 2 * LRU_WIDTH + ATTN_WIDTH,
                   2 * LRU_WIDTH + 2 * ATTN_WIDTH], axis=-1)
        y_a = rglru_mixer(x_lru, g_lru, lru_conv_w[l], lru_conv_b[l], lru_gate_w[l],
                          lru_gate_b[l], lru_lambda[l])
        y_b = neighbourhood_attention(q, k, v, attn_rpb[l])
        y = jnp.concatenate([rms_norm(y_a, lru_out_norm[l]), rms_norm(y_b, attn_out_norm[l])], axis=-1)
        h = h + y @ w_out_mix[l]
        h = h + 0.5 * swiglu(rms_norm(h, norm_ffn2[l]), ffn2_w_in[l], ffn2_w_out[l])
    return rms_norm(h, norm_final)


_drawn_inputs = setup_inputs


def setup_inputs(seed=0):
    import zlib

    import numpy as np

    out = dict(_drawn_inputs(seed))
    spreads = {}
    factors = {'lru_gate_b': 8.0, 'attn_rpb': 6.327, 'norm_ffn2': 3.789}
    for name, (base, spread) in spreads.items():
        noise = np.random.default_rng([zlib.crc32(name.encode()), seed]).standard_normal(out[name].shape)
        drawn = base * np.exp(spread * noise) if base else spread * noise
        out[name] = __import__('jax').numpy.asarray(drawn.astype(out[name].dtype))
    for name, factor in factors.items():
        out[name] = (out[name] * factor).astype(out[name].dtype)
    return out
```

```python
import math
from contextlib import ExitStack

import concourse.bass as bass
from concourse import mybir

P = 128
F32 = mybir.dt.float32
F32R = mybir.dt.float32r
ALU = mybir.AluOpType
ACT = mybir.ActivationFunctionType
AX_X = mybir.AxisListType.X

GRID_W = 64
WIN_ROWS = 8
WIN_COLS = 16
CONV_WIDTH = 4
EPS = 1e-6
RG_C = 8.0
MASKED = -1e30


def hybrid_encoder_block(
    nc: bass.Bass,
    x: bass.AP,
    norm_ffn1: bass.AP,
    ffn1_w_in: bass.AP,
    ffn1_w_out: bass.AP,
    norm_mix: bass.AP,
    w_in_mix: bass.AP,
    lru_conv_w: bass.AP,
    lru_conv_b: bass.AP,
    lru_gate_w: bass.AP,
    lru_gate_b: bass.AP,
    lru_lambda: bass.AP,
    attn_rpb: bass.AP,
    lru_out_norm: bass.AP,
    attn_out_norm: bass.AP,
    w_out_mix: bass.AP,
    norm_ffn2: bass.AP,
    ffn2_w_in: bass.AP,
    ffn2_w_out: bass.AP,
    norm_final: bass.AP,
    out: bass.AP,
):
    _, T, D = x.shape
    F = ffn1_w_out.shape[1]
    L = lru_conv_w.shape[2]
    A = w_in_mix.shape[2] // 3 - 2 * L // 3
    NH, NDR, NDC = attn_rpb.shape[1:]
    HD = A // NH
    DT, FT, LT, AT = D // P, F // P, L // P, A // P
    ROWS = T // GRID_W
    assert T == 256 and D == 2048 and L == A == D // 2 and HD == 64 and F % 512 == 0 and ROWS == 4

    CK, CN = 4, 512
    CT = CN // P
    UP_BLOCKS = F // CN
    UP_KS = DT // CK
    DOWN_KS = FT // CK
    MIX_BLOCKS = (2 * L + 3 * A) // (2 * CN)
    C_UP1 = 0
    C_DOWN1 = C_UP1 + UP_BLOCKS * 2 * UP_KS
    C_MIX_IN = C_DOWN1 + D // CN * DOWN_KS
    C_MIX_OUT = C_MIX_IN + MIX_BLOCKS * 2 * UP_KS
    C_UP2 = C_MIX_OUT + D // CN * UP_KS
    C_DOWN2 = C_UP2 + (C_DOWN1 - C_UP1)
    C_END = C_DOWN2 + (C_MIX_IN - C_DOWN1)
    NB = 8
    M_UP1 = NB
    M_DOWN1 = M_UP1 + UP_BLOCKS * 2 * CT
    M_MIX_IN = M_DOWN1 + DT
    M_MIX_OUT = M_MIX_IN + MIX_BLOCKS * 2 * CT
    M_UP2 = M_MIX_OUT + DT
    M_DOWN2 = M_UP2 + UP_BLOCKS * 2 * CT
    E_X, E_DOWN1, E_LRU, E_ATT = 0, DT, 2 * DT, 2 * DT + LT
    E_MIX, E_DOWN2, E_END = 3 * DT, 4 * DT, 5 * DT
    H_DOWN1, H_MIX, H_DOWN2 = 0, DT, 2 * DT
    V_FFN1, V_MIX, V_LRU, V_ATT, V_FFN2 = 0, DT, 2 * DT, 2 * DT + LT, 3 * DT
    N_FFN1, N_MIX, N_LRU, N_ATT, N_FFN2, N_FINAL = range(6)
    X0, G0, Q0, K0, V0 = 0, LT, 2 * LT, 2 * LT + AT, 2 * LT + 2 * AT
    XC0 = K0
    HLT = LT // 2

    QC = P // ROWS
    NJ = GRID_W // QC
    KS0 = 24
    KC = 40
    KR2 = 2 * KC
    NK = ROWS * KC
    HALF_WIN = WIN_COLS // 2
    HPB = 512 // NK
    HEAD_SLOT = [(head % 2) * (NH // 2) + head // 2 for head in range(NH)]
    SCORE_BANKS = [(par * (NH // 2) + a, par * (NH // 2) + min(a + HPB, NH // 2))
                   for par in range(2) for a in range(0, NH // 2, HPB)]
    DR0 = WIN_ROWS - ROWS
    NDRU = 2 * ROWS - 1
    PAD = 24
    PADW = 80

    ctx = ExitStack()
    with ctx:
        def sem(name):
            return ctx.enter_context(nc.semaphore(name))

        def sb(name, shape, dt=F32, stack=ctx):
            return stack.enter_context(nc.sbuf_tensor(name, shape, dt))

        rpb_padded = nc.dram_tensor("rpb_padded", [NH, NDRU, PADW], F32, kind="Internal").ap()

        psum = ctx.enter_context(nc.psum_tensor("psum", [P, NB, 512], F32))

        h = sb("h", [P, DT, T])
        w_raw = [sb(f"w_raw{s}", [P, CK, CN]) for s in range(2)]
        w_hi = [sb(f"w_hi{s}", [P, CK, CN], F32R) for s in range(2)]
        w_lo = [sb(f"w_lo{s}", [P, CK, CN], F32R) for s in range(2)]
        half_b = sb("half_b", [P, CT, T])
        gbuf = sb("gbuf", [P, CT, T])
        ubuf = sb("ubuf", [P, CT, T])
        sumsq = sb("sumsq", [P, T])
        std = sb("std", [P, T])
        rstd = sb("rstd", [P, T])
        ident = sb("ident", [P, P])
        ones = sb("ones", [P, P])
        eps = sb("eps", [P, 1])
        vec_rows = [sb(f"vec_rows{s}", [P, P]) for s in range(2)]
        vecs = sb("vecs", [P, 2 * P])
        lam_exp = sb("lam_exp", [P, 2 * LT])
        sp_s = sb("sp_s", [P, 2 * LT])
        sp_s2 = sb("sp_s2", [P, 2 * LT])
        sp_q = sb("sp_q", [P, 2 * LT])
        decay4 = sb("decay4", [P, 2 * LT])
        decay8n = sb("decay8n", [P, 2 * LT])
        mx = sb("mx", [P, NH])
        den = sb("den", [P, NH])
        rden = sb("rden", [P, NH])
        window = sb("window", [P, NJ, KC])

        with ExitStack() as region:
            act_t = sb("act_t", [P, DT, 2, T], F32R, region)
        with ExitStack() as region:
            v_nat = sb("v_nat", [KR2, NJ, 2, A], F32, region)
            with ExitStack() as inner:
                p_t = sb("p_t", [KR2, NH, 2, P], F32, inner)
            with ExitStack() as inner:
                v_keys = sb("v_keys", [P, NJ, 2, AT, KR2], F32, inner)
        with ExitStack() as region:
            lru_r = sb("lru_r", [P, HLT, 2, T], F32, region)
            lru_i = sb("lru_i", [P, HLT, 2, T], F32, region)
            lru_t = sb("lru_t", [P, HLT, 2, T], F32, region)
            lru_s = sb("lru_s", [P, HLT, 2, T], F32, region)
        with ExitStack() as region:
            fin_t = sb("fin_t", [P, DT, T], F32, region)
            fin_nat = sb("fin_nat", [P, 2, D], F32, region)
        sb("region_u", [P, DT, 2, T])
        with ExitStack() as region:
            hid_t = sb("hid_t", [P, FT, 2, T], F32R, region)
        with ExitStack() as region:
            x_nat = sb("x_nat", [P, 2, D], F32, region)
        with ExitStack() as region:
            proj = sb("proj", [P, 2 * LT + 3 * AT, T], F32, region)
            bias = sb("bias", [P, NJ, NH, NK], F32, region)
            prob = sb("prob", [P, NH, NK], F32, region)
            gate_w = sb("gate_w", [P, LT, 4, P], F32, region)
        sb("region_h", [P, FT, 2, T])

        raw_landed = [sem(f"raw_landed{s}") for s in range(2)]
        hi_split = sem("hi_split")
        lo_split = sem("lo_split")
        columns_done = sem("columns_done")
        half_copied = sem("half_copied")
        bank_free = sem("bank_free")
        silu_done = sem("silu_done")
        hidden_full = sem("hidden_full")
        hidden_hi = sem("hidden_hi")
        hidden_ready = sem("hidden_ready")
        h_written = sem("h_written")
        squared = sem("squared")
        sumsq_clear = sem("sumsq_clear")
        sumsq_done = sem("sumsq_done")
        stat_ready = sem("stat_ready")
        std_ready = sem("std_ready")
        rstd_ready = sem("rstd_ready")
        normed_full = sem("normed_full")
        normed_hi = sem("normed_hi")
        act_ready = sem("act_ready")
        x_landed = [sem(f"x_landed{s}") for s in range(2)]
        x_turned = sem("x_turned")
        consts = sem("consts")
        vec_clear = sem("vec_clear")
        vec_landed = sem("vec_landed")
        vec_turned = sem("vec_turned")
        vecs_ready = sem("vecs_ready")
        lam_exp_done = sem("lam_exp_done")
        decay_ready = sem("decay_ready")
        chain = sem("chain")
        pad_zero = sem("pad_zero")
        pad_done = sem("pad_done")
        bias_landed = sem("bias_landed")
        gate_zero = sem("gate_zero")
        gate_landed = sem("gate_landed")
        window_ready = sem("window_ready")
        keys_gathered = sem("keys_gathered")
        queries_gathered = sem("queries_gathered")
        v_turned = sem("v_turned")
        v_ready = sem("v_ready")
        scores_ready = sem("scores_ready")
        scores_read = sem("scores_read")
        centred = sem("centred")
        exp_done = sem("exp_done")
        prob_ready = sem("prob_ready")
        prob_turned = sem("prob_turned")
        prob_t_ready = sem("prob_t_ready")
        att_ready = sem("att_ready")
        att_read = sem("att_read")
        conv_done = sem("conv_done")
        gates_ready = sem("gates_ready")
        gates_read = sem("gates_read")
        tanh_done = sem("tanh_done")
        decay_done = sem("decay_done")
        sqrt_done = sem("sqrt_done")
        gelu_sq = sem("gelu_sq")
        gelu_arg = sem("gelu_arg")
        gelu_sig = sem("gelu_sig")
        gelu_done = sem("gelu_done")
        scanned = sem("scanned")
        lru_done = sem("lru_done")
        fin_scaled = sem("fin_scaled")
        fin_turned = sem("fin_turned")
        fin_out = sem("fin_out")
        out_written = sem("out_written")

        up1 = ffn1_w_in[0].rearrange("(t p) n -> p t n", p=P)
        up2 = ffn2_w_in[0].rearrange("(t p) n -> p t n", p=P)
        down1 = ffn1_w_out[0].rearrange("(t p) n -> p t n", p=P)
        down2 = ffn2_w_out[0].rearrange("(t p) n -> p t n", p=P)
        mix_in = w_in_mix[0].rearrange("(t p) n -> p t n", p=P)
        mix_out = w_out_mix[0].rearrange("(t p) n -> p t n", p=P)

        vec_parts = [[(norm_ffn1[0], DT), (norm_mix[0], DT), (norm_ffn2[0], DT), (norm_final, DT),
                      (lru_out_norm[0], LT), (attn_out_norm[0], AT), (lru_conv_b[0], LT)],
                     [(lru_conv_w[0].rearrange("w c -> (w c)"), CONV_WIDTH * LT),
                      (lru_gate_b[0].rearrange("z g h d -> (z g h d)"), 4 * LT),
                      (lru_lambda[0].rearrange("z c -> (z c)"), 2 * LT)]]
        N_PARTS = len(vec_parts[0]) + len(vec_parts[1])
        G_FFN1, G_MIX, G_FFN2, G_FINAL = 0, DT, 2 * DT, 3 * DT
        G_LRU, G_ATT, CONV_B = 4 * DT, 4 * DT + LT, 4 * DT + LT + AT
        CONV_W, GATE_B, LAMBDA = P, P + CONV_WIDTH * LT, P + (CONV_WIDTH + 4) * LT

        def vec(column):
            return vecs[:, column:column + 1]

        def grid(tile):
            return tile.rearrange("p (r c) -> p r c", c=GRID_W)

        def queries(part, tile, j):
            return proj[part, V0 + tile, j * P:(j + 1) * P]

        def reversed_columns(j):
            return slice((j + 1) * QC - 1, j * QC - 1 if j else None, -1)

        def flat(buf):
            return buf[:, :, :, :].rearrange("p c z t -> p (c z t)")

        block = ctx.enter_context(nc.Block())

        @block.sync
        def _(sp):
            for half in range(2):
                sp.dma_start(x_nat[:, half, :], x[0, half * P:(half + 1) * P, :]).then_inc(x_landed[half], 16)

            def load(weights, n, j, ks, column, fill=False):
                if not fill:
                    sp.wait_ge(lo_split, n - 1)
                sp.dma_start(w_raw[j % 2][:, :, :],
                             weights[:, CK * ks:CK * (ks + 1), bass.ds(column, CN)]
                             ).then_inc(raw_landed[j % 2], 16)

            def two_columns(weights, base, i, column, apart, fill=False):
                for ks in range(UP_KS):
                    for side in range(2):
                        j = 2 * ks + side
                        load(weights, base + 2 * UP_KS * i + j, j, ks, column + side * apart,
                             fill=fill and j < 2)

            def down(weights, base, n_ks, i):
                for group in range(2):
                    for ks in range(n_ks):
                        j = n_ks * group + ks
                        load(weights, base + 2 * n_ks * i + j, j, ks, (2 * i + group) * CN)

            two_columns(up1, C_UP1, 0, 0, F, fill=True)
            with sp.Fori(1, UP_BLOCKS) as i:
                two_columns(up1, C_UP1, i, i * CN, F)
            with sp.Fori(0, 2) as i:
                down(down1, C_DOWN1, DOWN_KS, i)
            with sp.Fori(0, MIX_BLOCKS) as i:
                two_columns(mix_in, C_MIX_IN, i, i * 2 * CN, CN)
            with sp.Fori(0, 2) as i:
                down(mix_out, C_MIX_OUT, UP_KS, i)
            with sp.Fori(0, UP_BLOCKS) as i:
                two_columns(up2, C_UP2, i, i * CN, F)
            with sp.Fori(0, 2) as i:
                down(down2, C_DOWN2, DOWN_KS, i)
            for half in range(2):
                sp.wait_ge(fin_out, 4 * (half + 1))
                sp.dma_start(out[0, half * P:(half + 1) * P, :], fin_nat[:, half, :]).then_inc(out_written, 16)
            sp.wait_ge(out_written, 32)

        @block.gpsimd
        def _(pool):
            pool.memset(ident[:, :], 0.0).then_inc(consts, 1)
            pool.memset(ones[:, :], 1.0).then_inc(consts, 1)
            pool.wait_ge(consts, 2)
            pool.affine_select(out=ident[:, :], in_=ident[:, :], compare_op=ALU.not_equal, fill=1.0,
                               base=0, pattern=[[-1, P]], channel_multiplier=1).then_inc(consts, 1)
            for s in range(2):
                pool.memset(vec_rows[s][:, :], 0.0).then_inc(vec_clear, 1)
            pool.wait_ge(vec_clear, 2)
            for s in range(2):
                at = 0
                for values, n in vec_parts[s]:
                    pool.dma_start(vec_rows[s][at:at + n, :], values.rearrange("(t p) -> t p", p=P)
                                   ).then_inc(vec_landed, 16)
                    at += n
            pool.memset(window[:, :, :], 0.0).then_inc(window_ready, 1)
            done = 1
            for j in range(NJ):
                low = min(KC, GRID_W - WIN_COLS - j * KS0)
                high = max(0, WIN_COLS - j * KS0)
                shift = j * (KS0 - QC)
                for r in range(ROWS):
                    row = window[r * QC:(r + 1) * QC, j, :]
                    pool.wait_ge(window_ready, done)
                    pool.affine_select(out=row[:, 0:low], in_=row[:, 0:low], compare_op=ALU.is_ge,
                                       fill=MASKED, base=shift + HALF_WIN - (QC - 1),
                                       pattern=[[1, low]], channel_multiplier=1).then_inc(window_ready, 1)
                    done += 1
                    pool.wait_ge(window_ready, done)
                    pool.affine_select(out=row[:, high:KC], in_=row[:, high:KC], compare_op=ALU.is_ge,
                                       fill=MASKED, base=HALF_WIN - 1 - shift - high + QC - 1,
                                       pattern=[[-1, KC - high]], channel_multiplier=-1).then_inc(window_ready, 1)
                    done += 1
            pool.wait_ge(vecs_ready, 1)
            pool.wait_ge(window_ready, done)
            pool.memset(vec_rows[0][:, :], 0.0).then_inc(pad_zero, 1)
            pool.wait_ge(pad_zero, 1)
            pool.dma_start(rpb_padded.rearrange("h r w -> (h r) w"), vec_rows[0][0:NH * NDRU, 0:PADW]
                           ).then_inc(pad_done, 16)
            pool.wait_ge(pad_done, 16)
            for par in range(2):
                heads = attn_rpb[0, :, DR0:DR0 + NDRU, :].rearrange("(t two) r c -> two t r c", two=2)[par]
                pool.dma_start(rpb_padded[par * (NH // 2):(par + 1) * (NH // 2), :, PAD:PAD + NDC], heads
                               ).then_inc(pad_done, 16)
            pool.wait_ge(pad_done, 48)
            pool.wait_ge(columns_done, CT * C_MIX_IN)
            pool.memset(gate_w[:, :, :, :], 0.0).then_inc(gate_zero, 1)
            for j in range(NJ):
                for r in range(ROWS):
                    for kr in range(ROWS):
                        start = (kr - r + ROWS - 1) * PADW + PAD + WIN_COLS - QC + j * (KS0 - QC)
                        sheared = bass.AP(rpb_padded.tensor, start, [[1, QC], [NDRU * PADW, NH], [1, KC]])
                        pool.dma_start(bias[r * QC:(r + 1) * QC, j, :, kr * KC:(kr + 1) * KC], sheared
                                       ).then_inc(bias_landed, 16)
            pool.wait_ge(gate_zero, 1)
            for zg in range(4):
                source = lru_gate_w[0, zg // 2, zg % 2].rearrange("(t two) i j -> two i t j", two=2)
                for par in range(2):
                    part = slice(HD * par, HD * (par + 1))
                    pool.dma_start(gate_w[part, :, zg, part], source[par]).then_inc(gate_landed, 16)

        @block.tensor
        def _(pe):
            def chunk(n, slot, rhs, k0, m, b0, first, last):
                pe.wait_ge(lo_split, n + 1)
                for c in range(CT):
                    if first:
                        pe.wait_ge(bank_free, m + c - (NB - 1))
                    for k in range(CK):
                        hi = w_hi[slot][:, k, c * P:(c + 1) * P]
                        lo = w_lo[slot][:, k, c * P:(c + 1) * P]
                        a_both = rhs[:, k0 + k, :, :].rearrange("p s t -> p (s t)")
                        a_hi = rhs[:, k0 + k, 0, :]
                        if last and k == CK - 1:
                            pe.matmul(psum[:, b0 + c, 0:T], lo, a_hi, start=False, stop=False)
                            mm = pe.matmul(psum[:, b0 + c, :], hi, a_both, start=False, stop=True)
                        else:
                            pe.matmul(psum[:, b0 + c, :], hi, a_both, start=first and k == 0, stop=False)
                            mm = pe.matmul(psum[:, b0 + c, 0:T], lo, a_hi, start=False, stop=False)
                    mm.then_inc(columns_done, 1)

            def two_columns(c_base, m_base, v_base, i):
                for ks in range(UP_KS):
                    pe.wait_ge(act_ready, v_base + CK * (ks + 1))
                    for side in range(2):
                        j = 2 * ks + side
                        chunk(c_base + 2 * UP_KS * i + j, j % 2, act_t, CK * ks,
                              m_base + 2 * CT * i + CT * side, CT * side, ks == 0, ks == UP_KS - 1)

            def down(c_base, m_base, n_ks, rhs, ready, ready_base, i):
                for group in range(2):
                    for ks in range(n_ks):
                        pe.wait_ge(ready, ready_base + CK * (ks + 1))
                        j = n_ks * group + ks
                        chunk(c_base + 2 * n_ks * i + j, j % 2, rhs, CK * ks,
                              m_base + 2 * CT * i + CT * group, CT * group, ks == 0, ks == n_ks - 1)

            def square_sum(e_end):
                pe.wait_ge(sumsq_done, e_end)
                pe.matmul(psum[:, NB - 1, 0:T], ones[:, :], sumsq[:, :], start=True, stop=True).then_inc(stat_ready, 1)

            pe.wait_ge(consts, 3)
            for half in range(2):
                pe.wait_ge(x_landed[half], 16)
            for t in range(DT):
                for half in range(2):
                    mm = pe.transpose(psum[:, t // 2, (t % 2) * T + half * P:(t % 2) * T + (half + 1) * P],
                                      x_nat[:, half, t * P:(t + 1) * P], ident[:, :])
                if t % 2 == 1:
                    mm.then_inc(x_turned, 1)
            pe.wait_ge(vec_landed, 16 * N_PARTS)
            pe.wait_ge(bank_free, NB)
            for s in range(2):
                mm = pe.transpose(psum[:, 1, s * P:(s + 1) * P], vec_rows[s][:, :], ident[:, :])
            mm.then_inc(vec_turned, 1)
            square_sum(E_X + DT)
            pe.wait_ge(vecs_ready, 1)

            with pe.Fori(0, UP_BLOCKS) as i:
                two_columns(C_UP1, M_UP1, V_FFN1, i)
            with pe.Fori(0, 2) as i:
                down(C_DOWN1, M_DOWN1, DOWN_KS, hid_t, hidden_ready, 0, i)
            square_sum(E_DOWN1 + DT)
            with pe.Fori(0, MIX_BLOCKS) as i:
                two_columns(C_MIX_IN, M_MIX_IN, V_MIX, i)

            for j in range(NJ):
                for m in range(2):
                    pe.wait_ge(keys_gathered, 2 * j + m + 1)
                    for t in range(AT):
                        mm = pe.transpose(psum[0:KR2, 4 * j + 2 * m + t // 4, (t % 4) * P:(t % 4 + 1) * P],
                                          v_keys[:, j, m, t, :], ident[:, :])
                        if t % 4 == 3:
                            mm.then_inc(v_turned, 1)
            pe.wait_ge(v_ready, NB)
            for j in range(NJ):
                pe.wait_ge(queries_gathered, NJ)
                if j > 0:
                    pe.wait_ge(att_read, AT * j)
                for g, (s0, s1) in enumerate(SCORE_BANKS):
                    for slot in range(s0, s1):
                        par, tile = divmod(slot, NH // 2)
                        part = slice(HD * par, HD * (par + 1))
                        keys = grid(proj[part, K0 + tile, :])[:, :, j * KS0:j * KS0 + KC]
                        mm = pe.matmul(psum[:, g, (slot - s0) * NK:(slot - s0 + 1) * NK],
                                       queries(part, tile, j), keys, start=True, stop=True)
                    mm.then_inc(scores_ready, 1)
                pe.wait_ge(prob_ready, j + 1)
                for head in range(NH):
                    for m in range(2):
                        col = ((head % 2) * 2 + m) * P
                        mm = pe.transpose(psum[0:KR2, head // 2, col:col + P],
                                          prob[:, HEAD_SLOT[head], m * KR2:(m + 1) * KR2], ident[:, :])
                    if head % 2 == 1:
                        mm.then_inc(prob_turned, 1)
                pe.wait_ge(prob_t_ready, NB * (j + 1))
                for head in range(NH):
                    part = slice(HD * (head % 2), HD * (head % 2 + 1))
                    pair = head // 2
                    for m in range(2):
                        mm = pe.matmul(psum[part, pair // 4, (pair % 4) * P:(pair % 4 + 1) * P],
                                       v_nat[:, j, m, head * HD:(head + 1) * HD], p_t[:, head, m, :],
                                       start=(m == 0), stop=(m == 1))
                    if head % 2 == 1:
                        mm.then_inc(att_ready, 1)

            pe.wait_ge(gate_landed, 16 * 8)
            pe.wait_ge(att_read, AT * NJ)
            for t in range(LT):
                pe.wait_ge(conv_done, t + 1)
                if t >= HLT:
                    pe.wait_ge(gates_read, 4 * (t - HLT + 1))
                for zg in range(4):
                    mm = pe.matmul(psum[:, 2 * (t % HLT) + zg // 2, (zg % 2) * T:(zg % 2 + 1) * T],
                                   gate_w[:, t, zg, :], proj[:, XC0 + t, :], start=True, stop=True)
                mm.then_inc(gates_ready, 1)

            square_sum(E_LRU + LT)
            square_sum(E_ATT + AT)
            with pe.Fori(0, 2) as i:
                down(C_MIX_OUT, M_MIX_OUT, UP_KS, act_t, act_ready, V_LRU, i)
            square_sum(E_MIX + DT)
            with pe.Fori(0, UP_BLOCKS) as i:
                two_columns(C_UP2, M_UP2, V_FFN2, i)
            with pe.Fori(0, 2) as i:
                down(C_DOWN2, M_DOWN2, DOWN_KS, hid_t, hidden_ready, FT, i)

            pe.wait_ge(sumsq_done, E_END)
            for half in range(2):
                mm = pe.matmul(psum[:, NB - 1, half:half + 1], sumsq[:, half * P:(half + 1) * P],
                               ones[:, 0:1], start=True, stop=True)
            mm.then_inc(stat_ready, 1)
            for half in range(2):
                for t in range(DT):
                    if half == 0:
                        pe.wait_ge(fin_scaled, t + 1)
                    if half == 1 and t == DT - 4:
                        pe.wait_ge(std_ready, N_FINAL + 1)
                    mm = pe.transpose(psum[:, 4 * half + t // 4, (t % 4) * P:(t % 4 + 1) * P],
                                      fin_t[:, t, half * P:(half + 1) * P], ident[:, :])
                    if t % 4 == 3:
                        mm.then_inc(fin_turned, 1)

        @block.scalar
        def _(act):
            def splits(n0, j0, j1, fill=False):
                for j in range(j0, j1):
                    act.wait_ge(raw_landed[j % 2], 8 * n0 + 16 * (j // 2 + 1))
                    if not fill:
                        act.wait_ge(columns_done, CT * (n0 + j - 1))
                    act.copy(w_hi[j % 2][:, :, :], w_raw[j % 2][:, :, :]).then_inc(hi_split, 1)

            def copy_halves(n, m, b0):
                for c in range(CT):
                    act.wait_ge(columns_done, CT * n + c + 1)
                    act.wait_ge(bank_free, m + c - (CT - 1))
                    act.copy(half_b[:, c, :], psum[:, b0 + c, T:2 * T]).then_inc(half_copied, 1)

            def hidden(c_base, m_base, f_base, i):
                n0 = c_base + 2 * UP_KS * i
                m = m_base + 2 * CT * i
                splits(n0, 2, 9)
                copy_halves(n0 + 2 * UP_KS - 2, m, 0)
                for c in range(CT):
                    act.wait_ge(bank_free, m + c + 1)
                    act.activation(gbuf[:, c, :], gbuf[:, c, :], ACT.Silu).then_inc(silu_done, 1)
                splits(n0, 9, 10)
                copy_halves(n0 + 2 * UP_KS - 1, m + CT, CT)
                for c in range(CT):
                    act.wait_ge(hidden_full, f_base + CT * i + c + 1)
                    act.copy(hid_t[:, CT * i + c, 0, :], ubuf[:, c, :]).then_inc(hidden_hi, 1)

            def squares(h_base, e_base, at):
                for c in range(CT):
                    act.wait_ge(h_written, h_base + at + c + 1)
                    act.wait_ge(sumsq_done, e_base + at + c - (CT - 1))
                    act.activation(gbuf[:, c, :], h[:, at + c, :], ACT.Square).then_inc(squared, 1)

            def down(c_base, m_base, h_base, e_base, n_ks, i, final=False):
                n0 = c_base + 2 * n_ks * i
                m = m_base + 2 * CT * i
                splits(n0, 2, n_ks + 2)
                copy_halves(n0 + n_ks - 1, m, 0)
                squares(h_base, e_base, 2 * CT * i)
                splits(n0, n_ks + 2, 2 * n_ks + (0 if final else 1))
                copy_halves(n0 + 2 * n_ks - 1, m + CT, CT)
                squares(h_base, e_base, 2 * CT * i + CT)
                if not final:
                    splits(n0, 2 * n_ks + 1, 2 * n_ks + 2)

            def norm(n, dims, v_base, count):
                act.wait_ge(stat_ready, n + 1)
                act.activation(std[:, :], psum[:, NB - 1, 0:T], ACT.Sqrt, bias=eps[:, 0:1], scale=1.0 / dims
                               ).then_inc(std_ready, 1)
                for t in range(count):
                    act.wait_ge(normed_full, v_base + t + 1)
                    act.copy(act_t[:, v_base % DT + t, 0, :], ubuf[:, t % CT, :]).then_inc(normed_hi, 1)

            for t in range(DT):
                act.wait_ge(bank_free, t // 2 + 1)
                if t >= CT:
                    act.wait_ge(sumsq_done, t - (CT - 1))
                act.activation(gbuf[:, t % CT, :], h[:, t, :], ACT.Square).then_inc(squared, 1)
            splits(0, 0, 2, fill=True)
            norm(N_FFN1, D, V_FFN1, DT)
            act.wait_ge(vecs_ready, 1)
            act.activation(lam_exp[:, :], vecs[:, LAMBDA:LAMBDA + 2 * LT], ACT.Abs).then_inc(lam_exp_done, 1)
            act.wait_ge(lam_exp_done, 1)
            act.activation(lam_exp[:, :], lam_exp[:, :], ACT.Exp, scale=-1.0).then_inc(lam_exp_done, 1)
            with act.Fori(0, UP_BLOCKS) as i:
                hidden(C_UP1, M_UP1, 0, i)
            with act.Fori(0, 2) as i:
                down(C_DOWN1, M_DOWN1, H_DOWN1, E_DOWN1, DOWN_KS, i)
            norm(N_MIX, D, V_MIX, DT)
            with act.Fori(0, MIX_BLOCKS) as i:
                n0 = C_MIX_IN + 2 * UP_KS * i
                m = M_MIX_IN + 2 * CT * i
                splits(n0, 2, 9)
                copy_halves(n0 + 2 * UP_KS - 2, m, 0)
                splits(n0, 9, 10)
                copy_halves(n0 + 2 * UP_KS - 1, m + CT, CT)

            for g in range(NB):
                act.wait_ge(v_turned, g + 1)
                act.copy(v_nat[:, g // 4, (g // 2) % 2, (g % 2) * 512:(g % 2 + 1) * 512], psum[0:KR2, g, :]
                         ).then_inc(v_ready, 1)
            for j in range(NJ):
                act.wait_ge(centred, j + 1)
                act.activation(prob[:, :, :], prob[:, :, :], ACT.Exp).then_inc(exp_done, 1)
                for g in range(NB):
                    act.wait_ge(prob_turned, NB * j + g + 1)
                    act.copy(p_t[:, 2 * g:2 * g + 2, :, :].rearrange("p h m q -> p (h m q)"), psum[0:KR2, g, :]
                             ).then_inc(prob_t_ready, 1)
                for t in range(AT):
                    act.wait_ge(att_ready, AT * j + 4 * (t // 4 + 1))
                    act.copy(grid(proj[:, Q0 + t, :])[:, :, reversed_columns(j)],
                             psum[:, t // 4, (t % 4) * P:(t % 4 + 1) * P].rearrange("p (r c) -> p r c", c=QC)
                             ).then_inc(att_read, 1)

            for hh in range(2):
                g_tiles = proj[:, G0 + HLT * hh:G0 + HLT * (hh + 1), :].rearrange("p c t -> p (c t)")
                gelu_tmp = flat(lru_t)[:, 0:HLT * T]
                if hh > 0:
                    act.wait_ge(lru_done, hh)
                act.activation(gelu_tmp, g_tiles, ACT.Square).then_inc(gelu_sq, 1)
                act.wait_ge(gelu_arg, hh + 1)
                act.activation(gelu_tmp, gelu_tmp, ACT.Sigmoid, scale=2.0 * (2.0 / math.pi) ** 0.5
                               ).then_inc(gelu_sig, 1)
                for c in range(HLT):
                    t = HLT * hh + c
                    act.wait_ge(gates_ready, t + 1)
                    for z in range(2):
                        for g, dest in enumerate((lru_r, lru_i)):
                            act.activation(dest[:, c, z, :], psum[:, 2 * c + z, g * T:(g + 1) * T], ACT.Sigmoid,
                                           bias=vec(GATE_B + (2 * z + g) * LT + t)).then_inc(gates_read, 1)
                act.wait_ge(gates_read, 4 * HLT * (hh + 1))
                act.wait_ge(gelu_done, hh + 1)
                act.wait_ge(decay_ready, 1)
                for c in range(HLT):
                    for z in range(2):
                        col = z * LT + HLT * hh + c
                        act.activation(lru_t[:, c, z, :], lru_r[:, c, z, :], ACT.Tanh,
                                       scale=decay4[:, col:col + 1]).then_inc(tanh_done, 1)
                act.wait_ge(tanh_done, 2 * HLT * (hh + 1))
                for c in range(HLT):
                    for z in range(2):
                        col = z * LT + HLT * hh + c
                        act.activation(lru_r[:, c, z, :], lru_r[:, c, z, :], ACT.Exp,
                                       scale=decay8n[:, col:col + 1]).then_inc(decay_done, 1)
                act.activation(flat(lru_s), flat(lru_t), ACT.Sqrt).then_inc(sqrt_done, 1)

            for n, (t0, e_base, v_base) in enumerate(((X0, E_LRU, V_LRU), (Q0, E_ATT, V_ATT))):
                act.wait_ge(lru_done, 2)
                for t in range(LT):
                    act.wait_ge(sumsq_done, e_base + t - (CT - 1))
                    act.activation(gbuf[:, t % CT, :], proj[:, t0 + t, :], ACT.Square).then_inc(squared, 1)
                norm(N_LRU + n, L, v_base, LT)
            with act.Fori(0, 2) as i:
                down(C_MIX_OUT, M_MIX_OUT, H_MIX, E_MIX, UP_KS, i)
            norm(N_FFN2, D, V_FFN2, DT)
            with act.Fori(0, UP_BLOCKS) as i:
                hidden(C_UP2, M_UP2, FT, i)
            down(C_DOWN2, M_DOWN2, H_DOWN2, E_DOWN2, DOWN_KS, 0)
            down(C_DOWN2, M_DOWN2, H_DOWN2, E_DOWN2, DOWN_KS, 1, final=True)
            act.wait_ge(stat_ready, N_FINAL + 1)
            act.activation(std[:, 0:2], psum[:, NB - 1, 0:2], ACT.Sqrt, bias=eps[:, 0:1], scale=1.0 / D
                           ).then_inc(std_ready, 1)

        @block.vector
        def _(dve):
            linked = [0]

            def link(ins):
                linked[0] += 1
                ins.then_inc(chain, 1)
                dve.wait_ge(chain, linked[0])

            def splits(n0, j0, j1, fill=False):
                for j in range(j0, j1):
                    dve.wait_ge(hi_split, n0 + j + 1)
                    dve.tensor_tensor(w_lo[j % 2][:, :, :], w_raw[j % 2][:, :, :],
                                      w_hi[j % 2][:, :, :].bitcast(F32), ALU.subtract).then_inc(lo_split, 1)

            def add_halves(m, b0, dest):
                for c in range(CT):
                    dve.wait_ge(half_copied, m + c + 1 - NB)
                    dve.tensor_tensor(dest[c], psum[:, b0 + c, 0:T], half_b[:, c, :], ALU.add
                                      ).then_inc(bank_free, 1)

            g_tiles4 = [gbuf[:, c, :] for c in range(CT)]
            u_tiles4 = [ubuf[:, c, :] for c in range(CT)]

            def hidden(c_base, m_base, f_base, i):
                n0 = c_base + 2 * UP_KS * i
                m = m_base + 2 * CT * i
                splits(n0, 2, 9)
                add_halves(m, 0, g_tiles4)
                splits(n0, 9, 10)
                add_halves(m + CT, CT, u_tiles4)
                for c in range(CT):
                    dve.wait_ge(silu_done, f_base + CT * i + c + 1)
                    dve.wait_ge(bank_free, m + CT + c + 1)
                    dve.tensor_tensor(ubuf[:, c, :], gbuf[:, c, :], ubuf[:, c, :], ALU.mult
                                      ).then_inc(hidden_full, 1)
                for c in range(CT):
                    dve.wait_ge(hidden_hi, f_base + CT * i + c + 1)
                    dve.tensor_tensor(hid_t[:, CT * i + c, 1, :], ubuf[:, c, :],
                                      hid_t[:, CT * i + c, 0, :].bitcast(F32), ALU.subtract
                                      ).then_inc(hidden_ready, 1)

            def sum_squares(e, first=False):
                for c in range(CT):
                    dve.wait_ge(squared, e + c + 1)
                    if not (first and c == 0):
                        dve.wait_ge(sumsq_done, e + c)
                    dve.tensor_tensor(sumsq[:, :], sumsq[:, :], gbuf[:, c, :], ALU.add).then_inc(sumsq_done, 1)

            def residual(m, b0, h_base, e_base, at, scale):
                add_halves(m, b0, u_tiles4)
                for c in range(CT):
                    dve.wait_ge(bank_free, m + c + 1)
                    dve.scalar_tensor_tensor(h[:, at + c, :], ubuf[:, c, :], scale, h[:, at + c, :],
                                             ALU.mult, ALU.add).then_inc(h_written, 1)
                sum_squares(e_base + at)

            def down(c_base, m_base, h_base, e_base, n_ks, scale, i, final=False):
                n0 = c_base + 2 * n_ks * i
                m = m_base + 2 * CT * i
                splits(n0, 2, n_ks + 2)
                residual(m, 0, h_base, e_base, 2 * CT * i, scale)
                splits(n0, n_ks + 2, 2 * n_ks + (0 if final else 1))
                residual(m + CT, CT, h_base, e_base, 2 * CT * i + CT, scale)
                if not final:
                    splits(n0, 2 * n_ks + 1, 2 * n_ks + 2)

            def norm(n, source, gain, v_base, count):
                dve.wait_ge(std_ready, n + 1)
                dve.reciprocal(rstd[:, :], std[:, :]).then_inc(rstd_ready, 1)
                dve.memset(sumsq[:, :], 0.0).then_inc(sumsq_clear, 1)
                dve.wait_ge(rstd_ready, n + 1)
                slot = v_base % DT

                def low(t):
                    dve.wait_ge(normed_hi, v_base + t + 1)
                    dve.tensor_tensor(act_t[:, slot + t, 1, :], ubuf[:, t % CT, :],
                                      act_t[:, slot + t, 0, :].bitcast(F32), ALU.subtract).then_inc(act_ready, 1)

                for t in range(count):
                    dve.scalar_tensor_tensor(ubuf[:, t % CT, :], source[:, t, :], vec(gain + t), rstd[:, :],
                                             ALU.mult, ALU.mult).then_inc(normed_full, 1)
                    if t > 0:
                        low(t - 1)
                low(count - 1)
                dve.wait_ge(sumsq_clear, n + 2)

            link(dve.memset(eps[:, :], EPS))
            dve.memset(sumsq[:, :], 0.0).then_inc(sumsq_clear, 1)
            dve.wait_ge(sumsq_clear, 1)
            for b in range(NB):
                dve.wait_ge(x_turned, b + 1)
                dve.tensor_copy(h[:, 2 * b:2 * b + 2, :].rearrange("p a t -> p (a t)"), psum[:, b, :]
                                ).then_inc(bank_free, 1)
            for t in range(0, DT, CT):
                sum_squares(E_X + t, first=(t == 0))
            dve.wait_ge(vec_turned, 1)
            dve.tensor_copy(vecs[:, :], psum[:, 1, 0:2 * P]).then_inc(vecs_ready, 1)
            splits(0, 0, 2)
            dve.wait_ge(vecs_ready, 1)
            norm(N_FFN1, h, G_FFN1, V_FFN1, DT)
            dve.wait_ge(lam_exp_done, 2)
            link(dve.tensor_scalar(sp_s2[:, :], lam_exp[:, :], 2.0, None, ALU.add))
            link(dve.reciprocal(sp_s[:, :], sp_s2[:, :]))
            link(dve.tensor_tensor(sp_s[:, :], sp_s[:, :], lam_exp[:, :], ALU.mult))
            link(dve.tensor_tensor(sp_s2[:, :], sp_s[:, :], sp_s[:, :], ALU.mult))
            link(dve.tensor_scalar(sp_q[:, :], sp_s2[:, :], 1.0 / 17, None, ALU.mult))
            for k in range(7, 0, -1):
                link(dve.scalar_tensor_tensor(sp_q[:, :], sp_q[:, :], 1.0 / (2 * k + 1), sp_s2[:, :],
                                              ALU.add, ALU.mult))
            link(dve.scalar_tensor_tensor(sp_q[:, :], sp_q[:, :], 1.0, sp_s[:, :], ALU.add, ALU.mult))
            link(dve.tensor_scalar(sp_s[:, :], vecs[:, LAMBDA:LAMBDA + 2 * LT], -1.0, 0.0, ALU.mult, ALU.max))
            link(dve.scalar_tensor_tensor(sp_s[:, :], sp_q[:, :], 2.0, sp_s[:, :], ALU.mult, ALU.add))
            link(dve.tensor_scalar(decay4[:, :], sp_s[:, :], RG_C / 2, None, ALU.mult))
            dve.tensor_scalar(decay8n[:, :], sp_s[:, :], -RG_C, None, ALU.mult).then_inc(decay_ready, 1)

            with dve.Fori(0, UP_BLOCKS) as i:
                hidden(C_UP1, M_UP1, 0, i)
            with dve.Fori(0, 2) as i:
                down(C_DOWN1, M_DOWN1, H_DOWN1, E_DOWN1, DOWN_KS, 0.5, i)
            norm(N_MIX, h, G_MIX, V_MIX, DT)
            with dve.Fori(0, MIX_BLOCKS) as i:
                n0 = C_MIX_IN + 2 * UP_KS * i
                m = M_MIX_IN + 2 * CT * i
                splits(n0, 2, 9)
                add_halves(m, 0, [proj[:, 2 * CT * i + c, :] for c in range(CT)])
                splits(n0, 9, 10)
                add_halves(m + CT, CT, [proj[:, 2 * CT * i + CT + c, :] for c in range(CT)])

            dve.wait_ge(bank_free, M_MIX_OUT)
            for j in range(NJ):
                for m in range(2):
                    v_rows = proj[:, V0:V0 + AT, :].rearrange("p t (r c) -> p t r c", c=GRID_W)
                    dve.tensor_copy(v_keys[:, j, m, :, :].rearrange("p t (r c) -> p t r c", c=KC),
                                    v_rows[:, :, 2 * m:2 * m + 2, j * KS0:j * KS0 + KC]).then_inc(keys_gathered, 1)
            dve.wait_ge(keys_gathered, 2 * NJ)
            for j in range(NJ):
                q_rows = proj[:, Q0:Q0 + AT, :].rearrange("p t (r c) -> p t r c", c=GRID_W)
                dve.tensor_copy(proj[:, V0:V0 + AT, j * P:(j + 1) * P].rearrange("p t (r c) -> p t r c", c=QC),
                                q_rows[:, :, :, reversed_columns(j)]).then_inc(queries_gathered, 1)
            dve.wait_ge(bias_landed, 16 * NJ * ROWS * ROWS)
            dve.wait_ge(window_ready, 1 + 2 * NJ * ROWS)
            for j in range(NJ):
                rows = bias[:, j, :, :].rearrange("p h (r k) -> p (h r) k", k=KC)
                link(dve.tensor_tensor(rows, rows, window[:, j, :].unsqueeze(1).broadcast_to([P, NH * ROWS, KC]),
                                       ALU.add))
            flat_prob = prob[:, :, :].rearrange("p h k -> p (h k)")
            for j in range(NJ):
                flat_bias = bias[:, j, :, :].rearrange("p h k -> p (h k)")
                if j > 0:
                    dve.wait_ge(prob_turned, NB * j)
                for g, (s0, s1) in enumerate(SCORE_BANKS):
                    dve.wait_ge(scores_ready, len(SCORE_BANKS) * j + g + 1)
                    dve.scalar_tensor_tensor(flat_prob[:, s0 * NK:s1 * NK], psum[:, g, 0:(s1 - s0) * NK],
                                             HD ** -0.5, flat_bias[:, s0 * NK:s1 * NK], ALU.mult, ALU.add
                                             ).then_inc(scores_read, 1)
                dve.wait_ge(scores_read, len(SCORE_BANKS) * (j + 1))
                link(dve.tensor_reduce(mx[:, :], prob[:, :, :], AX_X, ALU.max))
                dve.tensor_tensor(prob[:, :, :], prob[:, :, :], mx[:, :].unsqueeze(2).broadcast_to([P, NH, NK]),
                                  ALU.subtract).then_inc(centred, 1)
                dve.wait_ge(exp_done, j + 1)
                link(dve.tensor_reduce(den[:, :], prob[:, :, :], AX_X, ALU.add))
                link(dve.reciprocal(rden[:, :], den[:, :]))
                dve.tensor_tensor(prob[:, :, :], prob[:, :, :], rden[:, :].unsqueeze(2).broadcast_to([P, NH, NK]),
                                  ALU.mult).then_inc(prob_ready, 1)

            dve.wait_ge(att_ready, AT * NJ)
            for t in range(LT):
                xin, xc = proj[:, X0 + t, :], proj[:, XC0 + t, :]
                centre = CONV_WIDTH // 2
                link(dve.tensor_scalar(xc, xin, vec(CONV_W + centre * LT + t), vec(CONV_B + t),
                                       ALU.mult, ALU.add))
                for w in (0, 1, 3):
                    d = w - centre
                    o0, o1 = max(0, -d), T - max(0, d)
                    tap = dve.scalar_tensor_tensor(xc[:, o0:o1], xin[:, o0 + d:o1 + d], vec(CONV_W + w * LT + t),
                                                   xc[:, o0:o1], ALU.mult, ALU.add)
                    if w < 3:
                        link(tap)
                    else:
                        tap.then_inc(conv_done, 1)

            for hh in range(2):
                g_tiles = proj[:, G0 + HLT * hh:G0 + HLT * (hh + 1), :].rearrange("p c t -> p (c t)")
                x_tiles = proj[:, X0 + HLT * hh:X0 + HLT * (hh + 1), :]
                xc_tiles = proj[:, XC0 + HLT * hh:XC0 + HLT * (hh + 1), :]
                gelu_tmp = flat(lru_t)[:, 0:HLT * T]
                dve.wait_ge(gelu_sq, hh + 1)
                link(dve.tensor_scalar(gelu_tmp, gelu_tmp, 0.044715, 1.0, ALU.mult, ALU.add))
                dve.tensor_tensor(gelu_tmp, gelu_tmp, g_tiles, ALU.mult).then_inc(gelu_arg, 1)
                dve.wait_ge(gelu_sig, hh + 1)
                dve.tensor_tensor(g_tiles, g_tiles, gelu_tmp, ALU.mult).then_inc(gelu_done, 1)
                dve.wait_ge(conv_done, LT)
                dve.wait_ge(gates_read, 4 * HLT * (hh + 1))
                for z in range(2):
                    link(dve.tensor_tensor(lru_i[:, :, z, :], lru_i[:, :, z, :], xc_tiles, ALU.mult))
                dve.wait_ge(decay_done, 2 * HLT * (hh + 1))
                dve.wait_ge(sqrt_done, hh + 1)
                link(dve.scalar_tensor_tensor(flat(lru_s), flat(lru_r), 1.0, flat(lru_s), ALU.add, ALU.mult))
                link(dve.tensor_tensor(flat(lru_i), flat(lru_s), flat(lru_i), ALU.mult))
                link(dve.scalar_tensor_tensor(flat(lru_t), flat(lru_r), 1.0, flat(lru_t), ALU.add, ALU.mult))
                link(dve.tensor_scalar(flat(lru_r), flat(lru_t), -1.0, 1.0, ALU.mult, ALU.add))
                for c in range(HLT):
                    dve.tensor_tensor_scan(lru_s[:, c, 0, :], lru_r[:, c, 0, :], lru_i[:, c, 0, :], 0.0,
                                           ALU.mult, ALU.add).then_inc(scanned, 1)
                    dve.tensor_tensor_scan(lru_s[:, c, 1, ::-1], lru_r[:, c, 1, ::-1], lru_i[:, c, 1, ::-1], 0.0,
                                           ALU.mult, ALU.add).then_inc(scanned, 1)
                dve.wait_ge(scanned, 2 * HLT * (hh + 1))
                link(dve.tensor_tensor(x_tiles, lru_s[:, :, 0, :], lru_s[:, :, 1, :], ALU.add))
                dve.wait_ge(gelu_done, hh + 1)
                flat_x = x_tiles.rearrange("p c t -> p (c t)")
                dve.tensor_tensor(flat_x, flat_x, g_tiles, ALU.mult).then_inc(lru_done, 1)

            for n, (t0, e_base, v_base, gain) in enumerate(((X0, E_LRU, V_LRU, G_LRU), (Q0, E_ATT, V_ATT, G_ATT))):
                for t in range(0, LT, CT):
                    sum_squares(e_base + t)
                norm(N_LRU + n, proj[:, t0:t0 + LT, :], gain, v_base, LT)
            with dve.Fori(0, 2) as i:
                down(C_MIX_OUT, M_MIX_OUT, H_MIX, E_MIX, UP_KS, 1.0, i)
            norm(N_FFN2, h, G_FFN2, V_FFN2, DT)
            with dve.Fori(0, UP_BLOCKS) as i:
                hidden(C_UP2, M_UP2, FT, i)
            down(C_DOWN2, M_DOWN2, H_DOWN2, E_DOWN2, DOWN_KS, 0.5, 0)
            down(C_DOWN2, M_DOWN2, H_DOWN2, E_DOWN2, DOWN_KS, 0.5, 1, final=True)
            for t in range(DT):
                dve.tensor_scalar(fin_t[:, t, :], h[:, t, :], vec(G_FINAL + t), None, ALU.mult
                                  ).then_inc(fin_scaled, 1)
            dve.wait_ge(std_ready, N_FINAL + 1)
            link(dve.reciprocal(rstd[:, 0:2], std[:, 0:2]))
            for half in range(2):
                for g in range(4):
                    dve.wait_ge(fin_turned, 4 * half + g + 1)
                    dve.tensor_scalar(fin_nat[:, half, 512 * g:512 * (g + 1)], psum[:, 4 * half + g, :],
                                      rstd[:, half:half + 1], None, ALU.mult).then_inc(fin_out, 1)


_INS = ['x', 'norm_ffn1', 'ffn1_w_in', 'ffn1_w_out', 'norm_mix', 'w_in_mix', 'lru_conv_w', 'lru_conv_b',
        'lru_gate_w', 'lru_gate_b', 'lru_lambda', 'attn_rpb', 'lru_out_norm', 'attn_out_norm', 'w_out_mix',
        'norm_ffn2', 'ffn2_w_in', 'ffn2_w_out', 'norm_final']
_OUTS = [((1, 256, 2048), 'float32')]


def kernel(**inputs):
    import numpy as _np
    import concourse.bacc as _bacc
    from concourse import mybir as _mybir
    from concourse.bass_utils import run_bass_kernel_spmd as _run

    nc = _bacc.Bacc("TRN2", target_bir_lowering=False, num_devices=1)
    arrays, args = {}, []
    for name in _INS:
        a = _np.ascontiguousarray(inputs[name])
        arrays[f"in_{name}_dram"] = a
        args.append(nc.dram_tensor(f"in_{name}_dram", a.shape, _mybir.dt.from_np(a.dtype), kind="ExternalInput").ap())
    for i, (shape, dtype) in enumerate(_OUTS):
        dt = _mybir.dt.from_np(_np.dtype(dtype))
        args.append(nc.dram_tensor(f"out_{i}_dram", shape, dt, kind="ExternalOutput").ap())
    hybrid_encoder_block(nc, *args)
    r = _run(nc, [arrays], core_ids=[0])
    got = tuple(r.results[0][f"out_{i}_dram"] for i in range(len(_OUTS)))
    return got[0]
```

```python
import math
from contextlib import ExitStack

import concourse.bass as bass
from concourse import mybir

P = 128
F32 = mybir.dt.float32
F32R = mybir.dt.float32r
ALU = mybir.AluOpType
ACT = mybir.ActivationFunctionType
AX_X = mybir.AxisListType.X
RADD = bass.bass_isa.ReduceOp.add

GRID_W = 64
WIN_ROWS = 8
WIN_COLS = 16
CONV_WIDTH = 4
EPS = 1e-6
RG_C = 8.0
MASKED = -1e30


def hybrid_encoder_block(
    nc: bass.Bass,
    x: bass.AP,
    norm_ffn1: bass.AP,
    ffn1_w_in: bass.AP,
    ffn1_w_out: bass.AP,
    norm_mix: bass.AP,
    w_in_mix: bass.AP,
    lru_conv_w: bass.AP,
    lru_conv_b: bass.AP,
    lru_gate_w: bass.AP,
    lru_gate_b: bass.AP,
    lru_lambda: bass.AP,
    attn_rpb: bass.AP,
    lru_out_norm: bass.AP,
    attn_out_norm: bass.AP,
    w_out_mix: bass.AP,
    norm_ffn2: bass.AP,
    ffn2_w_in: bass.AP,
    ffn2_w_out: bass.AP,
    norm_final: bass.AP,
    out: bass.AP,
):
    _, T, D = x.shape
    F = ffn1_w_out.shape[1]
    L = lru_conv_w.shape[2]
    A = w_in_mix.shape[2] // 3 - 2 * L // 3
    NH, NDR, NDC = attn_rpb.shape[1:]
    HD = A // NH
    DT, FT, LT, AT = D // P, F // P, L // P, A // P
    ROWS = T // GRID_W
    assert T == 256 and D == 2048 and L == A == D // 2 and HD == 64 and F % 512 == 0 and ROWS == 4

    CK, CN = 4, 512
    CT = CN // P
    UP_BLOCKS = F // CN
    UP_KS = DT // CK
    DOWN_KS = FT // CK
    MIX_BLOCKS = (2 * L + 3 * A) // (2 * CN)
    C_UP1 = 0
    C_DOWN1 = C_UP1 + UP_BLOCKS * 2 * UP_KS
    C_MIX_IN = C_DOWN1 + D // CN * DOWN_KS
    C_MIX_OUT = C_MIX_IN + MIX_BLOCKS * 2 * UP_KS
    C_UP2 = C_MIX_OUT + D // CN * UP_KS
    C_DOWN2 = C_UP2 + (C_DOWN1 - C_UP1)
    C_END = C_DOWN2 + (C_MIX_IN - C_DOWN1)
    NB = 8
    M_UP1 = NB
    M_DOWN1 = M_UP1 + UP_BLOCKS * 2 * CT
    M_MIX_IN = M_DOWN1 + DT
    M_MIX_OUT = M_MIX_IN + MIX_BLOCKS * 2 * CT
    M_UP2 = M_MIX_OUT + DT
    M_DOWN2 = M_UP2 + UP_BLOCKS * 2 * CT
    E_X, E_DOWN1, E_LRU, E_ATT = 0, DT, 2 * DT, 2 * DT + LT
    E_MIX, E_DOWN2, E_END = 3 * DT, 4 * DT, 5 * DT
    H_DOWN1, H_MIX, H_DOWN2 = 0, DT, 2 * DT
    V_FFN1, V_MIX, V_LRU, V_ATT, V_FFN2 = 0, DT, 2 * DT, 2 * DT + LT, 3 * DT
    N_FFN1, N_MIX, N_LRU, N_ATT, N_FFN2, N_FINAL = range(6)
    X0, G0, Q0, K0, V0 = 0, LT, 2 * LT, 2 * LT + AT, 2 * LT + 2 * AT
    XC0 = K0
    HLT = LT // 2

    QC = P // ROWS
    NJ = GRID_W // QC
    KS0 = 24
    KC = 40
    KR2 = 2 * KC
    NK = ROWS * KC
    HALF_WIN = WIN_COLS // 2
    HPB = 512 // NK
    HEAD_SLOT = [(head % 2) * (NH // 2) + head // 2 for head in range(NH)]
    SCORE_BANKS = [(par * (NH // 2) + a, par * (NH // 2) + min(a + HPB, NH // 2))
                   for par in range(2) for a in range(0, NH // 2, HPB)]
    DR0 = WIN_ROWS - ROWS
    NDRU = 2 * ROWS - 1
    PAD = 24
    PADW = 80

    ctx = ExitStack()
    with ctx:
        def sem(name):
            return ctx.enter_context(nc.semaphore(name))

        def sb(name, shape, dt=F32, stack=ctx):
            return stack.enter_context(nc.sbuf_tensor(name, shape, dt))

        rpb_padded = nc.dram_tensor("rpb_padded", [NH, NDRU, PADW], F32, kind="Internal").ap()

        psum = ctx.enter_context(nc.psum_tensor("psum", [P, NB, 512], F32))

        h = sb("h", [P, DT, T])
        w_raw = [sb(f"w_raw{s}", [P, CK, CN]) for s in range(2)]
        w_hi = [sb(f"w_hi{s}", [P, CK, CN], F32R) for s in range(2)]
        w_lo = [sb(f"w_lo{s}", [P, CK, CN], F32R) for s in range(2)]
        half_b = sb("half_b", [P, CT, T])
        gbuf = sb("gbuf", [P, CT, T])
        ubuf = sb("ubuf", [P, CT, T])
        sumsq = sb("sumsq", [P, T])
        stat = sb("stat", [P, T])
        std = sb("std", [P, T])
        rstd = sb("rstd", [P, T])
        ident = sb("ident", [P, P])
        ones = sb("ones", [P, P])
        eps = sb("eps", [P, 1])
        vec_rows = [sb(f"vec_rows{s}", [P, P]) for s in range(2)]
        vecs = sb("vecs", [P, 2 * P])
        lam_exp = sb("lam_exp", [P, 2 * LT])
        sp_s = sb("sp_s", [P, 2 * LT])
        sp_s2 = sb("sp_s2", [P, 2 * LT])
        sp_q = sb("sp_q", [P, 2 * LT])
        decay4 = sb("decay4", [P, 2 * LT])
        decay8n = sb("decay8n", [P, 2 * LT])
        mx = sb("mx", [P, NH])
        den = sb("den", [P, NH])
        rden = sb("rden", [P, NH])
        window = sb("window", [P, NJ, KC])

        with ExitStack() as region:
            act_t = sb("act_t", [P, DT, 2, T], F32R, region)
        with ExitStack() as region:
            v_nat = sb("v_nat", [KR2, NJ, 2, A], F32, region)
            with ExitStack() as inner:
                p_t = sb("p_t", [KR2, NH, 2, P], F32, inner)
            with ExitStack() as inner:
                v_keys = sb("v_keys", [P, NJ, 2, AT, KR2], F32, inner)
        with ExitStack() as region:
            lru_r = sb("lru_r", [P, HLT, 2, T], F32, region)
            lru_i = sb("lru_i", [P, HLT, 2, T], F32, region)
            lru_t = sb("lru_t", [P, HLT, 2, T], F32, region)
            lru_s = sb("lru_s", [P, HLT, 2, T], F32, region)
        with ExitStack() as region:
            fin_t = sb("fin_t", [P, DT, T], F32, region)
            fin_nat = sb("fin_nat", [P, 2, D], F32, region)
        sb("region_u", [P, DT, 2, T])
        with ExitStack() as region:
            hid_t = sb("hid_t", [P, FT, 2, T], F32R, region)
        with ExitStack() as region:
            x_nat = sb("x_nat", [P, 2, D], F32, region)
        with ExitStack() as region:
            proj = sb("proj", [P, 2 * LT + 3 * AT, T], F32, region)
            with ExitStack() as inner:
                bias = sb("bias", [P, NJ, NH, NK], F32, inner)
                prob = sb("prob", [P, NH, NK], F32, inner)
                gate_w = sb("gate_w", [P, LT, 4, P], F32, inner)
            with ExitStack() as inner:
                mix_t = sb("mix_t", [P, DT, 2, T], F32R, inner)
        sb("region_h", [P, FT, 2, T])

        raw_landed = [sem(f"raw_landed{s}") for s in range(2)]
        hi_split = sem("hi_split")
        lo_split = sem("lo_split")
        columns_done = sem("columns_done")
        half_copied = sem("half_copied")
        bank_free = sem("bank_free")
        gate_scaled = sem("gate_scaled")
        up_scaled = sem("up_scaled")
        silu_done = sem("silu_done")
        act_hi = sem("act_hi")
        proj_scaled = sem("proj_scaled")
        hidden_full = sem("hidden_full")
        hidden_hi = sem("hidden_hi")
        hidden_ready = sem("hidden_ready")
        h_written = sem("h_written")
        squared = sem("squared")
        sumsq_clear = sem("sumsq_clear")
        sumsq_done = sem("sumsq_done")
        stat_ready = sem("stat_ready")
        std_ready = sem("std_ready")
        rstd_ready = sem("rstd_ready")
        normed_full = sem("normed_full")
        normed_hi = sem("normed_hi")
        act_ready = sem("act_ready")
        x_landed = [[sem(f"x_landed{half}_{q}") for q in range(4)] for half in range(2)]
        x_turned = sem("x_turned")
        consts = sem("consts")
        vec_clear = sem("vec_clear")
        vec_landed = sem("vec_landed")
        vec_turned = sem("vec_turned")
        vecs_ready = sem("vecs_ready")
        lam_exp_done = sem("lam_exp_done")
        decay_ready = sem("decay_ready")
        chain = sem("chain")
        pad_zero = sem("pad_zero")
        pad_done = sem("pad_done")
        bias_landed = sem("bias_landed")
        gate_zero = sem("gate_zero")
        gate_landed = sem("gate_landed")
        window_ready = sem("window_ready")
        keys_gathered = sem("keys_gathered")
        queries_gathered = sem("queries_gathered")
        v_turned = sem("v_turned")
        v_ready = sem("v_ready")
        scores_ready = sem("scores_ready")
        scores_read = sem("scores_read")
        centred = sem("centred")
        exp_done = sem("exp_done")
        prob_ready = sem("prob_ready")
        prob_turned = sem("prob_turned")
        prob_t_ready = sem("prob_t_ready")
        att_ready = sem("att_ready")
        att_read = sem("att_read")
        conv_done = sem("conv_done")
        gates_ready = sem("gates_ready")
        gates_read = sem("gates_read")
        tanh_done = sem("tanh_done")
        decay_done = sem("decay_done")
        sqrt_done = sem("sqrt_done")
        gelu_sq = sem("gelu_sq")
        gelu_arg = sem("gelu_arg")
        gelu_sig = sem("gelu_sig")
        gelu_done = sem("gelu_done")
        scanned = sem("scanned")
        lru_done = sem("lru_done")
        fin_scaled = sem("fin_scaled")
        fin_turned = sem("fin_turned")
        fin_out = sem("fin_out")
        out_written = sem("out_written")

        up1 = ffn1_w_in[0].rearrange("(t p) n -> p t n", p=P)
        up2 = ffn2_w_in[0].rearrange("(t p) n -> p t n", p=P)
        down1 = ffn1_w_out[0].rearrange("(t p) n -> p t n", p=P)
        down2 = ffn2_w_out[0].rearrange("(t p) n -> p t n", p=P)
        mix_in = w_in_mix[0].rearrange("(t p) n -> p t n", p=P)
        mix_out = w_out_mix[0].rearrange("(t p) n -> p t n", p=P)

        vec_parts = [[(norm_ffn1[0], DT), (norm_mix[0], DT), (norm_ffn2[0], DT), (norm_final, DT),
                      (lru_out_norm[0], LT), (attn_out_norm[0], AT), (lru_conv_b[0], LT)],
                     [(lru_conv_w[0].rearrange("w c -> (w c)"), CONV_WIDTH * LT),
                      (lru_gate_b[0].rearrange("z g h d -> (z g h d)"), 4 * LT),
                      (lru_lambda[0].rearrange("z c -> (z c)"), 2 * LT)]]
        N_PARTS = len(vec_parts[0]) + len(vec_parts[1])
        G_FFN1, G_MIX, G_FFN2, G_FINAL = 0, DT, 2 * DT, 3 * DT
        G_LRU, G_ATT, CONV_B = 4 * DT, 4 * DT + LT, 4 * DT + LT + AT
        CONV_W, GATE_B, LAMBDA = P, P + CONV_WIDTH * LT, P + (CONV_WIDTH + 4) * LT

        def vec(column):
            return vecs[:, bass.ds(column, 1)]

        def grid(tile):
            return tile.rearrange("p (r c) -> p r c", c=GRID_W)

        def queries(part, tile, j):
            return proj[part, V0 + tile, j * P:(j + 1) * P]

        def reversed_columns(j):
            return slice((j + 1) * QC - 1, j * QC - 1 if j else None, -1)

        def flat(buf):
            return buf[:, :, :, :].rearrange("p c z t -> p (c z t)")

        block = ctx.enter_context(nc.Block())

        @block.sync
        def _(sp):
            for q in range(4):
                for half in range(2):
                    cols = slice(q * D // 4, (q + 1) * D // 4)
                    sp.dma_start(x_nat[:, half, cols], x[0, half * P:(half + 1) * P, cols]
                                 ).then_inc(x_landed[half][q], 16)

            def load(weights, n, j, ks, column, fill=False):
                if not fill:
                    sp.wait_ge(lo_split, n - 1)
                sp.dma_start(w_raw[j % 2][:, :, :],
                             weights[:, CK * ks:CK * (ks + 1), bass.ds(column, CN)]
                             ).then_inc(raw_landed[j % 2], 16)

            def two_columns(weights, base, i, column, apart, fill=False):
                for ks in range(UP_KS):
                    for side in range(2):
                        j = 2 * ks + side
                        load(weights, base + 2 * UP_KS * i + j, j, ks, column + side * apart,
                             fill=fill and j < 2)

            def down(weights, base, n_ks, i):
                for group in range(2):
                    for ks in range(n_ks):
                        j = n_ks * group + ks
                        load(weights, base + 2 * n_ks * i + j, j, ks, (2 * i + group) * CN)

            two_columns(up1, C_UP1, 0, 0, F, fill=True)
            with sp.Fori(1, UP_BLOCKS) as i:
                two_columns(up1, C_UP1, i, i * CN, F)
            with sp.Fori(0, 2) as i:
                down(down1, C_DOWN1, DOWN_KS, i)
            with sp.Fori(0, MIX_BLOCKS) as i:
                two_columns(mix_in, C_MIX_IN, i, i * 2 * CN, CN)
            with sp.Fori(0, 2) as i:
                down(mix_out, C_MIX_OUT, UP_KS, i)
            with sp.Fori(0, UP_BLOCKS) as i:
                two_columns(up2, C_UP2, i, i * CN, F)
            with sp.Fori(0, 2) as i:
                down(down2, C_DOWN2, DOWN_KS, i)
            for half in range(2):
                sp.wait_ge(fin_out, 4 * (half + 1))
                sp.dma_start(out[0, half * P:(half + 1) * P, :], fin_nat[:, half, :]).then_inc(out_written, 16)
            sp.wait_ge(out_written, 32)

        @block.gpsimd
        def _(pool):
            pool.memset(ident[:, :], 0.0).then_inc(consts, 1)
            pool.memset(ones[:, :], 1.0).then_inc(consts, 1)
            pool.wait_ge(consts, 2)
            pool.affine_select(out=ident[:, :], in_=ident[:, :], compare_op=ALU.not_equal, fill=1.0,
                               base=0, pattern=[[-1, P]], channel_multiplier=1).then_inc(consts, 1)
            for s in range(2):
                pool.memset(vec_rows[s][:, :], 0.0).then_inc(vec_clear, 1)
            pool.wait_ge(vec_clear, 2)
            for s in range(2):
                at = 0
                for values, n in vec_parts[s]:
                    pool.dma_start(vec_rows[s][at:at + n, :], values.rearrange("(t p) -> t p", p=P)
                                   ).then_inc(vec_landed, 16)
                    at += n
            pool.memset(window[:, :, :], 0.0).then_inc(window_ready, 1)
            done = 1
            for j in range(NJ):
                low = min(KC, GRID_W - WIN_COLS - j * KS0)
                high = max(0, WIN_COLS - j * KS0)
                shift = j * (KS0 - QC)
                for r in range(ROWS):
                    row = window[r * QC:(r + 1) * QC, j, :]
                    pool.wait_ge(window_ready, done)
                    pool.affine_select(out=row[:, 0:low], in_=row[:, 0:low], compare_op=ALU.is_ge,
                                       fill=MASKED, base=shift + HALF_WIN - (QC - 1),
                                       pattern=[[1, low]], channel_multiplier=1).then_inc(window_ready, 1)
                    done += 1
                    pool.wait_ge(window_ready, done)
                    pool.affine_select(out=row[:, high:KC], in_=row[:, high:KC], compare_op=ALU.is_ge,
                                       fill=MASKED, base=HALF_WIN - 1 - shift - high + QC - 1,
                                       pattern=[[-1, KC - high]], channel_multiplier=-1).then_inc(window_ready, 1)
                    done += 1

            def square_sum(n, e_end):
                pool.wait_ge(sumsq_done, e_end)
                pool.partition_all_reduce(stat[:, :], sumsq[:, :], P, RADD).then_inc(stat_ready, 1)
                pool.wait_ge(stat_ready, n + 1)

            pool.wait_ge(vecs_ready, 1)
            pool.wait_ge(window_ready, done)
            pool.memset(vec_rows[0][:, :], 0.0).then_inc(pad_zero, 1)
            pool.wait_ge(pad_zero, 1)
            pool.dma_start(rpb_padded.rearrange("h r w -> (h r) w"), vec_rows[0][0:NH * NDRU, 0:PADW]
                           ).then_inc(pad_done, 16)
            pool.wait_ge(pad_done, 16)
            for par in range(2):
                heads = attn_rpb[0, :, DR0:DR0 + NDRU, :].rearrange("(t two) r c -> two t r c", two=2)[par]
                pool.dma_start(rpb_padded[par * (NH // 2):(par + 1) * (NH // 2), :, PAD:PAD + NDC], heads
                               ).then_inc(pad_done, 16)
            pool.wait_ge(pad_done, 48)
            square_sum(N_FFN1, E_X + DT)
            square_sum(N_MIX, E_DOWN1 + DT)
            pool.wait_ge(columns_done, CT * C_MIX_IN)
            pool.memset(gate_w[:, :, :, :], 0.0).then_inc(gate_zero, 1)
            for j in range(NJ):
                for r in range(ROWS):
                    for kr in range(ROWS):
                        start = (kr - r + ROWS - 1) * PADW + PAD + WIN_COLS - QC + j * (KS0 - QC)
                        sheared = bass.AP(rpb_padded.tensor, start, [[1, QC], [NDRU * PADW, NH], [1, KC]])
                        pool.dma_start(bias[r * QC:(r + 1) * QC, j, :, kr * KC:(kr + 1) * KC], sheared
                                       ).then_inc(bias_landed, 16)
            pool.wait_ge(gate_zero, 1)
            for zg in range(4):
                source = lru_gate_w[0, zg // 2, zg % 2].rearrange("(t two) i j -> two i t j", two=2)
                for par in range(2):
                    part = slice(HD * par, HD * (par + 1))
                    pool.dma_start(gate_w[part, :, zg, part], source[par]).then_inc(gate_landed, 16)
            square_sum(N_LRU, E_LRU + LT)
            square_sum(N_ATT, E_ATT + AT)
            square_sum(N_FFN2, E_MIX + DT)

        @block.tensor
        def _(pe):
            def chunk(n, slot, rhs, k0, m, b0, first, last):
                pe.wait_ge(lo_split, n + 1)
                for c in range(CT):
                    if first:
                        pe.wait_ge(bank_free, m + c - (NB - 1))
                    for k in range(CK):
                        hi = w_hi[slot][:, k, c * P:(c + 1) * P]
                        lo = w_lo[slot][:, k, c * P:(c + 1) * P]
                        a_both = rhs[:, k0 + k, :, :].rearrange("p s t -> p (s t)")
                        a_hi = rhs[:, k0 + k, 0, :]
                        if last and k == CK - 1:
                            pe.matmul(psum[:, b0 + c, 0:T], lo, a_hi, start=False, stop=False)
                            mm = pe.matmul(psum[:, b0 + c, :], hi, a_both, start=False, stop=True)
                        else:
                            pe.matmul(psum[:, b0 + c, :], hi, a_both, start=first and k == 0, stop=False)
                            mm = pe.matmul(psum[:, b0 + c, 0:T], lo, a_hi, start=False, stop=False)
                    mm.then_inc(columns_done, 1)

            def two_columns(c_base, m_base, v_base, i):
                for ks in range(UP_KS):
                    pe.wait_ge(act_ready, v_base + CK * (ks + 1))
                    for side in range(2):
                        j = 2 * ks + side
                        chunk(c_base + 2 * UP_KS * i + j, j % 2, act_t, CK * ks,
                              m_base + 2 * CT * i + CT * side, CT * side, ks == 0, ks == UP_KS - 1)

            def down(c_base, m_base, n_ks, rhs, ready, ready_base, i):
                for group in range(2):
                    for ks in range(n_ks):
                        pe.wait_ge(ready, ready_base + CK * (ks + 1))
                        j = n_ks * group + ks
                        chunk(c_base + 2 * n_ks * i + j, j % 2, rhs, CK * ks,
                              m_base + 2 * CT * i + CT * group, CT * group, ks == 0, ks == n_ks - 1)

            pe.wait_ge(consts, 3)
            pe.wait_ge(vec_landed, 16 * N_PARTS)
            for s in range(2):
                mm = pe.transpose(psum[:, NB - 1, s * P:(s + 1) * P], vec_rows[s][:, :], ident[:, :])
            mm.then_inc(vec_turned, 1)
            for t in range(DT):
                if t % 4 == 0:
                    for half in range(2):
                        pe.wait_ge(x_landed[half][t // 4], 16)
                if t == DT - 2:
                    pe.wait_ge(vecs_ready, 1)
                for half in range(2):
                    mm = pe.transpose(psum[:, t // 2, (t % 2) * T + half * P:(t % 2) * T + (half + 1) * P],
                                      x_nat[:, half, t * P:(t + 1) * P], ident[:, :])
                if t % 2 == 1:
                    mm.then_inc(x_turned, 1)

            with pe.Fori(0, UP_BLOCKS) as i:
                two_columns(C_UP1, M_UP1, V_FFN1, i)
            with pe.Fori(0, 2) as i:
                down(C_DOWN1, M_DOWN1, DOWN_KS, hid_t, hidden_ready, 0, i)
            with pe.Fori(0, MIX_BLOCKS) as i:
                two_columns(C_MIX_IN, M_MIX_IN, V_MIX, i)

            for j in range(NJ):
                for m in range(2):
                    pe.wait_ge(keys_gathered, 2 * j + m + 1)
                    for t in range(AT):
                        mm = pe.transpose(psum[0:KR2, 4 * j + 2 * m + t // 4, (t % 4) * P:(t % 4 + 1) * P],
                                          v_keys[:, j, m, t, :], ident[:, :])
                        if t % 4 == 3:
                            mm.then_inc(v_turned, 1)
            pe.wait_ge(v_ready, NB)
            for j in range(NJ):
                pe.wait_ge(queries_gathered, NJ)
                if j > 0:
                    pe.wait_ge(att_read, AT * j)
                for g, (s0, s1) in enumerate(SCORE_BANKS):
                    for slot in range(s0, s1):
                        par, tile = divmod(slot, NH // 2)
                        part = slice(HD * par, HD * (par + 1))
                        keys = grid(proj[part, K0 + tile, :])[:, :, j * KS0:j * KS0 + KC]
                        mm = pe.matmul(psum[:, g, (slot - s0) * NK:(slot - s0 + 1) * NK],
                                       queries(part, tile, j), keys, start=True, stop=True)
                    mm.then_inc(scores_ready, 1)
                pe.wait_ge(prob_ready, j + 1)
                for head in range(NH):
                    for m in range(2):
                        col = ((head % 2) * 2 + m) * P
                        mm = pe.transpose(psum[0:KR2, head // 2, col:col + P],
                                          prob[:, HEAD_SLOT[head], m * KR2:(m + 1) * KR2], ident[:, :])
                    if head % 2 == 1:
                        mm.then_inc(prob_turned, 1)
                pe.wait_ge(prob_t_ready, NB * (j + 1))
                for head in range(NH):
                    part = slice(HD * (head % 2), HD * (head % 2 + 1))
                    pair = head // 2
                    for m in range(2):
                        mm = pe.matmul(psum[part, pair // 4, (pair % 4) * P:(pair % 4 + 1) * P],
                                       v_nat[:, j, m, head * HD:(head + 1) * HD], p_t[:, head, m, :],
                                       start=(m == 0), stop=(m == 1))
                    if head % 2 == 1:
                        mm.then_inc(att_ready, 1)

            pe.wait_ge(gate_landed, 16 * 8)
            pe.wait_ge(att_read, AT * NJ)
            for t in range(LT):
                pe.wait_ge(conv_done, t + 1)
                if t >= HLT:
                    pe.wait_ge(gates_read, 4 * (t - HLT + 1))
                for zg in range(4):
                    mm = pe.matmul(psum[:, 2 * (t % HLT) + zg // 2, (zg % 2) * T:(zg % 2 + 1) * T],
                                   gate_w[:, t, zg, :], proj[:, XC0 + t, :], start=True, stop=True)
                mm.then_inc(gates_ready, 1)

            with pe.Fori(0, 2) as i:
                down(C_MIX_OUT, M_MIX_OUT, UP_KS, mix_t, act_ready, V_LRU, i)
            with pe.Fori(0, UP_BLOCKS) as i:
                two_columns(C_UP2, M_UP2, V_FFN2, i)
            with pe.Fori(0, 2) as i:
                down(C_DOWN2, M_DOWN2, DOWN_KS, hid_t, hidden_ready, FT, i)

            pe.wait_ge(sumsq_done, E_END)
            for half in range(2):
                mm = pe.matmul(psum[:, NB - 1, half:half + 1], sumsq[:, half * P:(half + 1) * P],
                               ones[:, 0:1], start=True, stop=True)
            mm.then_inc(stat_ready, 1)
            for half in range(2):
                for t in range(DT):
                    if half == 0:
                        pe.wait_ge(fin_scaled, t + 1)
                    if half == 1 and t == DT - 4:
                        pe.wait_ge(std_ready, N_FINAL + 1)
                    mm = pe.transpose(psum[:, 4 * half + t // 4, (t % 4) * P:(t % 4 + 1) * P],
                                      fin_t[:, t, half * P:(half + 1) * P], ident[:, :])
                    if t % 4 == 3:
                        mm.then_inc(fin_turned, 1)

        @block.scalar
        def _(act):
            def splits(n0, j0, j1, fill=False):
                for j in range(j0, j1):
                    act.wait_ge(raw_landed[j % 2], 8 * n0 + 16 * (j // 2 + 1))
                    if not fill:
                        act.wait_ge(columns_done, CT * (n0 + j - 1))
                    act.copy(w_hi[j % 2][:, :, :], w_raw[j % 2][:, :, :]).then_inc(hi_split, 1)

            def copy_halves(n, m, b0):
                for c in range(CT):
                    act.wait_ge(columns_done, CT * n + c + 1)
                    act.wait_ge(bank_free, m + c - (CT - 1))
                    act.copy(half_b[:, c, :], psum[:, b0 + c, T:2 * T]).then_inc(half_copied, 1)

            def hidden(c_base, m_base, f_base, i):
                n0 = c_base + 2 * UP_KS * i
                m = m_base + 2 * CT * i
                splits(n0, 4, 8)
                copy_halves(n0 + 2 * UP_KS - 2, m, 0)
                splits(n0, 8, 9)
                copy_halves(n0 + 2 * UP_KS - 1, m + CT, CT)
                splits(n0, 9, 10)
                for c in range(CT):
                    act.wait_ge(gate_scaled, f_base + CT * i + c + 1)
                    act.activation(gbuf[:, c, :], gbuf[:, c, :], ACT.Silu).then_inc(silu_done, 1)
                splits(n0, 10, 11)
                for c in range(CT):
                    act.wait_ge(hidden_full, f_base + CT * i + c + 1)
                    act.copy(hid_t[:, CT * i + c, 0, :], ubuf[:, c, :]).then_inc(hidden_hi, 1)
                splits(n0, 11, 12)

            def high(t, gain, ready, count):
                act.wait_ge(ready, count)
                act.activation(act_t[:, t, 0, :], h[:, t, :], ACT.Copy, scale=vec(gain + t)).then_inc(act_hi, 1)

            def squares(h_base, e_base, at):
                for c in range(CT):
                    act.wait_ge(h_written, h_base + at + c + 1)
                    act.wait_ge(sumsq_done, e_base + at + c - (CT - 1))
                    act.activation(gbuf[:, c, :], h[:, at + c, :], ACT.Square).then_inc(squared, 1)

            def down(c_base, m_base, h_base, e_base, gain, n_ks, i, final=False):
                n0 = c_base + 2 * n_ks * i
                m = m_base + 2 * CT * i
                for group in range(2):
                    end = n_ks * (group + 1)
                    at = 2 * CT * i + CT * group
                    last = final and group == 1
                    splits(n0, 4 if group == 0 else n_ks + 3, end + (0 if last else 2))
                    copy_halves(n0 + end - 1, m + CT * group, CT * group)
                    if not last:
                        splits(n0, end + 2, end + 3)
                    if gain is not None:
                        for c in range(CT):
                            high(at + c, gain, h_written, h_base + at + c + 1)
                    squares(h_base, e_base, at)
                if not final:
                    splits(n0, 2 * n_ks + 3, 2 * n_ks + 4)

            def deviation(n, dims):
                act.wait_ge(stat_ready, n + 1)
                act.activation(std[:, :], stat[:, :], ACT.Sqrt, bias=eps[:, 0:1], scale=1.0 / dims
                               ).then_inc(std_ready, 1)

            def norm(n, dims, v_base, count):
                deviation(n, dims)
                for t in range(count):
                    act.wait_ge(normed_full, v_base - V_LRU + t + 1)
                    act.copy(mix_t[:, v_base - V_LRU + t, 0, :], ubuf[:, t % CT, :]).then_inc(normed_hi, 1)

            act.wait_ge(vecs_ready, 1)
            for t in range(DT):
                high(t, G_FFN1, bank_free, t // 2 + 1)
                if t == CT - 1:
                    splits(0, 0, 2, fill=True)
            for t in range(DT):
                if t >= CT:
                    act.wait_ge(sumsq_done, t - (CT - 1))
                act.activation(gbuf[:, t % CT, :], h[:, t, :], ACT.Square).then_inc(squared, 1)
            splits(0, 2, 4)
            act.activation(lam_exp[:, :], vecs[:, LAMBDA:LAMBDA + 2 * LT], ACT.Abs).then_inc(lam_exp_done, 1)
            act.wait_ge(lam_exp_done, 1)
            act.activation(lam_exp[:, :], lam_exp[:, :], ACT.Exp, scale=-1.0).then_inc(lam_exp_done, 1)
            deviation(N_FFN1, D)
            with act.Fori(0, UP_BLOCKS) as i:
                hidden(C_UP1, M_UP1, 0, i)
            for i in range(2):
                down(C_DOWN1, M_DOWN1, H_DOWN1, E_DOWN1, G_MIX, DOWN_KS, i)
            deviation(N_MIX, D)

            def project(i, last=False):
                n0 = C_MIX_IN + 2 * UP_KS * i
                m = M_MIX_IN + 2 * CT * i
                splits(n0, 4, 9)
                copy_halves(n0 + 2 * UP_KS - 2, m, 0)
                splits(n0, 9, 10)
                copy_halves(n0 + 2 * UP_KS - 1, m + CT, CT)
                if not last:
                    splits(n0, 10, 12)

            with act.Fori(0, MIX_BLOCKS - 1) as i:
                project(i)
            project(MIX_BLOCKS - 1, last=True)

            for g in range(NB):
                act.wait_ge(v_turned, g + 1)
                act.copy(v_nat[:, g // 4, (g // 2) % 2, (g % 2) * 512:(g % 2 + 1) * 512], psum[0:KR2, g, :]
                         ).then_inc(v_ready, 1)
            for j in range(NJ):
                act.wait_ge(centred, j + 1)
                act.activation(prob[:, :, :], prob[:, :, :], ACT.Exp).then_inc(exp_done, 1)
                for g in range(NB):
                    act.wait_ge(prob_turned, NB * j + g + 1)
                    act.copy(p_t[:, 2 * g:2 * g + 2, :, :].rearrange("p h m q -> p (h m q)"), psum[0:KR2, g, :]
                             ).then_inc(prob_t_ready, 1)
                for t in range(AT):
                    act.wait_ge(att_ready, AT * j + 4 * (t // 4 + 1))
                    act.copy(grid(proj[:, Q0 + t, :])[:, :, reversed_columns(j)],
                             psum[:, t // 4, (t % 4) * P:(t % 4 + 1) * P].rearrange("p (r c) -> p r c", c=QC)
                             ).then_inc(att_read, 1)

            for hh in range(2):
                g_tiles = proj[:, G0 + HLT * hh:G0 + HLT * (hh + 1), :].rearrange("p c t -> p (c t)")
                gelu_tmp = flat(lru_t)[:, 0:HLT * T]
                if hh > 0:
                    act.wait_ge(lru_done, hh)
                act.activation(gelu_tmp, g_tiles, ACT.Square).then_inc(gelu_sq, 1)
                act.wait_ge(gelu_arg, hh + 1)
                act.activation(gelu_tmp, gelu_tmp, ACT.Sigmoid, scale=2.0 * (2.0 / math.pi) ** 0.5
                               ).then_inc(gelu_sig, 1)
                for c in range(HLT):
                    t = HLT * hh + c
                    act.wait_ge(gates_ready, t + 1)
                    for z in range(2):
                        for g, dest in enumerate((lru_r, lru_i)):
                            act.activation(dest[:, c, z, :], psum[:, 2 * c + z, g * T:(g + 1) * T], ACT.Sigmoid,
                                           bias=vec(GATE_B + (2 * z + g) * LT + t)).then_inc(gates_read, 1)
                act.wait_ge(gates_read, 4 * HLT * (hh + 1))
                act.wait_ge(gelu_done, hh + 1)
                act.wait_ge(decay_ready, 1)
                for c in range(HLT):
                    for z in range(2):
                        col = z * LT + HLT * hh + c
                        act.activation(lru_t[:, c, z, :], lru_r[:, c, z, :], ACT.Tanh,
                                       scale=decay4[:, col:col + 1]).then_inc(tanh_done, 1)
                act.wait_ge(tanh_done, 2 * HLT * (hh + 1))
                for c in range(HLT):
                    for z in range(2):
                        col = z * LT + HLT * hh + c
                        act.activation(lru_r[:, c, z, :], lru_r[:, c, z, :], ACT.Exp,
                                       scale=decay8n[:, col:col + 1]).then_inc(decay_done, 1)
                act.activation(flat(lru_s), flat(lru_t), ACT.Sqrt).then_inc(sqrt_done, 1)

            for n, (t0, e_base, v_base) in enumerate(((X0, E_LRU, V_LRU), (Q0, E_ATT, V_ATT))):
                act.wait_ge(lru_done, 2)
                for t in range(LT):
                    act.wait_ge(sumsq_done, e_base + t - (CT - 1))
                    act.activation(gbuf[:, t % CT, :], proj[:, t0 + t, :], ACT.Square).then_inc(squared, 1)
                norm(N_LRU + n, L, v_base, LT)
            splits(C_MIX_OUT, 2, 4)
            for i in range(2):
                down(C_MIX_OUT, M_MIX_OUT, H_MIX, E_MIX, G_FFN2, UP_KS, i)
            deviation(N_FFN2, D)
            with act.Fori(0, UP_BLOCKS) as i:
                hidden(C_UP2, M_UP2, FT, i)
            down(C_DOWN2, M_DOWN2, H_DOWN2, E_DOWN2, None, DOWN_KS, 0)
            down(C_DOWN2, M_DOWN2, H_DOWN2, E_DOWN2, None, DOWN_KS, 1, final=True)
            act.wait_ge(stat_ready, N_FINAL + 1)
            act.activation(std[:, 0:2], psum[:, NB - 1, 0:2], ACT.Sqrt, bias=eps[:, 0:1], scale=1.0 / D
                           ).then_inc(std_ready, 1)

        @block.vector
        def _(dve):
            linked = [0]

            def link(ins):
                linked[0] += 1
                ins.then_inc(chain, 1)
                dve.wait_ge(chain, linked[0])

            def splits(n0, j0, j1, fill=False):
                for j in range(j0, j1):
                    dve.wait_ge(hi_split, n0 + j + 1)
                    dve.tensor_tensor(w_lo[j % 2][:, :, :], w_raw[j % 2][:, :, :],
                                      w_hi[j % 2][:, :, :].bitcast(F32), ALU.subtract).then_inc(lo_split, 1)

            def add_halves(m, b0, dest):
                for c in range(CT):
                    dve.wait_ge(half_copied, m + c + 1 - NB)
                    dve.tensor_tensor(dest[c], psum[:, b0 + c, 0:T], half_b[:, c, :], ALU.add
                                      ).then_inc(bank_free, 1)

            g_tiles4 = [gbuf[:, c, :] for c in range(CT)]
            u_tiles4 = [ubuf[:, c, :] for c in range(CT)]

            def hidden(c_base, m_base, f_base, i):
                n0 = c_base + 2 * UP_KS * i
                m = m_base + 2 * CT * i
                f = f_base + CT * i
                splits(n0, 4, 8)
                add_halves(m, 0, g_tiles4)
                splits(n0, 8, 9)
                add_halves(m + CT, CT, u_tiles4)
                for c in range(CT):
                    dve.wait_ge(bank_free, m + c + 1)
                    dve.tensor_tensor(gbuf[:, c, :], gbuf[:, c, :], rstd[:, :], ALU.mult).then_inc(gate_scaled, 1)
                splits(n0, 9, 10)
                for c in range(CT):
                    dve.wait_ge(bank_free, m + CT + c + 1)
                    dve.tensor_tensor(ubuf[:, c, :], ubuf[:, c, :], rstd[:, :], ALU.mult).then_inc(up_scaled, 1)
                for c in range(CT):
                    dve.wait_ge(silu_done, f + c + 1)
                    dve.wait_ge(up_scaled, f + c + 1)
                    dve.tensor_tensor(ubuf[:, c, :], gbuf[:, c, :], ubuf[:, c, :], ALU.mult
                                      ).then_inc(hidden_full, 1)
                splits(n0, 10, 11)
                for c in range(CT):
                    dve.wait_ge(hidden_hi, f + c + 1)
                    dve.tensor_tensor(hid_t[:, CT * i + c, 1, :], ubuf[:, c, :],
                                      hid_t[:, CT * i + c, 0, :].bitcast(F32), ALU.subtract
                                      ).then_inc(hidden_ready, 1)
                splits(n0, 11, 12)

            def sum_squares(e, first=False):
                for c in range(CT):
                    dve.wait_ge(squared, e + c + 1)
                    if not (first and c == 0):
                        dve.wait_ge(sumsq_done, e + c)
                    dve.tensor_tensor(sumsq[:, :], sumsq[:, :], gbuf[:, c, :], ALU.add).then_inc(sumsq_done, 1)

            def low(count, t, gain):
                dve.wait_ge(act_hi, count)
                dve.scalar_tensor_tensor(act_t[:, t, 1, :], h[:, t, :], vec(gain + t),
                                         act_t[:, t, 0, :].bitcast(F32), ALU.mult, ALU.subtract
                                         ).then_inc(act_ready, 1)

            def down(c_base, m_base, h_base, e_base, hi_base, gain, n_ks, scale, i, final=False):
                n0 = c_base + 2 * n_ks * i
                m = m_base + 2 * CT * i
                for group in range(2):
                    end = n_ks * (group + 1)
                    at = 2 * CT * i + CT * group
                    last = final and group == 1
                    splits(n0, 4 if group == 0 else n_ks + 3, end + (0 if last else 2))
                    add_halves(m + CT * group, CT * group, u_tiles4)
                    for c in range(CT):
                        dve.wait_ge(bank_free, m + CT * group + c + 1)
                        dve.scalar_tensor_tensor(h[:, at + c, :], ubuf[:, c, :], scale, h[:, at + c, :],
                                                 ALU.mult, ALU.add).then_inc(h_written, 1)
                    if not last:
                        splits(n0, end + 2, end + 3)
                    for c in range(CT):
                        if gain is None:
                            dve.wait_ge(h_written, h_base + at + c + 1)
                            dve.tensor_scalar(fin_t[:, at + c, :], h[:, at + c, :], vec(G_FINAL + at + c), None,
                                              ALU.mult).then_inc(fin_scaled, 1)
                        else:
                            low(hi_base + at + c + 1, at + c, gain)
                    sum_squares(e_base + at)
                if not final:
                    splits(n0, 2 * n_ks + 3, 2 * n_ks + 4)

            def scales(n):
                dve.wait_ge(std_ready, n + 1)
                dve.reciprocal(rstd[:, :], std[:, :]).then_inc(rstd_ready, 1)
                dve.memset(sumsq[:, :], 0.0).then_inc(sumsq_clear, 1)
                dve.wait_ge(rstd_ready, n + 1)
                dve.wait_ge(sumsq_clear, n + 2)

            def norm(n, source, gain, v_base, count):
                scales(n)
                slot = v_base - V_LRU

                def low_mix(t):
                    dve.wait_ge(normed_hi, slot + t + 1)
                    dve.tensor_tensor(mix_t[:, slot + t, 1, :], ubuf[:, t % CT, :],
                                      mix_t[:, slot + t, 0, :].bitcast(F32), ALU.subtract).then_inc(act_ready, 1)

                for t in range(count):
                    dve.scalar_tensor_tensor(ubuf[:, t % CT, :], source[:, t, :], vec(gain + t), rstd[:, :],
                                             ALU.mult, ALU.mult).then_inc(normed_full, 1)
                    if t > 0:
                        low_mix(t - 1)
                low_mix(count - 1)

            link(dve.memset(eps[:, :], EPS))
            dve.memset(sumsq[:, :], 0.0).then_inc(sumsq_clear, 1)
            dve.wait_ge(sumsq_clear, 1)
            dve.wait_ge(vec_turned, 1)
            dve.tensor_copy(vecs[:, :], psum[:, NB - 1, 0:2 * P]).then_inc(vecs_ready, 1)
            dve.wait_ge(vecs_ready, 1)
            for b in range(NB):
                dve.wait_ge(x_turned, b + 1)
                dve.tensor_copy(h[:, 2 * b:2 * b + 2, :].rearrange("p a t -> p (a t)"), psum[:, b, :]
                                ).then_inc(bank_free, 1)
                dve.wait_ge(bank_free, b + 1)
                for t in (2 * b, 2 * b + 1):
                    low(t + 1, t, G_FFN1)
                if b == 1:
                    splits(0, 0, 2)
            for t in range(0, DT, CT):
                sum_squares(E_X + t, first=(t == 0))
            splits(0, 2, 4)
            dve.wait_ge(lam_exp_done, 2)
            link(dve.tensor_scalar(sp_s2[:, :], lam_exp[:, :], 2.0, None, ALU.add))
            link(dve.reciprocal(sp_s[:, :], sp_s2[:, :]))
            link(dve.tensor_tensor(sp_s[:, :], sp_s[:, :], lam_exp[:, :], ALU.mult))
            link(dve.tensor_tensor(sp_s2[:, :], sp_s[:, :], sp_s[:, :], ALU.mult))
            link(dve.tensor_scalar(sp_q[:, :], sp_s2[:, :], 1.0 / 17, None, ALU.mult))
            for k in range(7, 0, -1):
                link(dve.scalar_tensor_tensor(sp_q[:, :], sp_q[:, :], 1.0 / (2 * k + 1), sp_s2[:, :],
                                              ALU.add, ALU.mult))
            link(dve.scalar_tensor_tensor(sp_q[:, :], sp_q[:, :], 1.0, sp_s[:, :], ALU.add, ALU.mult))
            link(dve.tensor_scalar(sp_s[:, :], vecs[:, LAMBDA:LAMBDA + 2 * LT], -1.0, 0.0, ALU.mult, ALU.max))
            link(dve.scalar_tensor_tensor(sp_s[:, :], sp_q[:, :], 2.0, sp_s[:, :], ALU.mult, ALU.add))
            link(dve.tensor_scalar(decay4[:, :], sp_s[:, :], RG_C / 2, None, ALU.mult))
            dve.tensor_scalar(decay8n[:, :], sp_s[:, :], -RG_C, None, ALU.mult).then_inc(decay_ready, 1)

            scales(N_FFN1)
            with dve.Fori(0, UP_BLOCKS) as i:
                hidden(C_UP1, M_UP1, 0, i)
            with dve.Fori(0, 2) as i:
                down(C_DOWN1, M_DOWN1, H_DOWN1, E_DOWN1, DT, G_MIX, DOWN_KS, 0.5, i)
            scales(N_MIX)

            def project(i, last=False):
                n0 = C_MIX_IN + 2 * UP_KS * i
                m = M_MIX_IN + 2 * CT * i
                splits(n0, 4, 9)
                for side in range(2):
                    add_halves(m + CT * side, CT * side,
                               [proj[:, 2 * CT * i + CT * side + c, :] for c in range(CT)])
                    for c in range(CT):
                        tile = proj[:, 2 * CT * i + CT * side + c, :]
                        dve.wait_ge(bank_free, m + CT * side + c + 1)
                        dve.tensor_tensor(tile, tile, rstd[:, :], ALU.mult).then_inc(proj_scaled, 1)
                    if side == 0:
                        splits(n0, 9, 10)
                if not last:
                    splits(n0, 10, 12)

            with dve.Fori(0, MIX_BLOCKS - 1) as i:
                project(i)
            project(MIX_BLOCKS - 1, last=True)

            dve.wait_ge(proj_scaled, 2 * LT + 3 * AT)
            for j in range(NJ):
                for m in range(2):
                    v_rows = proj[:, V0:V0 + AT, :].rearrange("p t (r c) -> p t r c", c=GRID_W)
                    dve.tensor_copy(v_keys[:, j, m, :, :].rearrange("p t (r c) -> p t r c", c=KC),
                                    v_rows[:, :, 2 * m:2 * m + 2, j * KS0:j * KS0 + KC]).then_inc(keys_gathered, 1)
            dve.wait_ge(keys_gathered, 2 * NJ)
            for j in range(NJ):
                q_rows = proj[:, Q0:Q0 + AT, :].rearrange("p t (r c) -> p t r c", c=GRID_W)
                dve.tensor_copy(proj[:, V0:V0 + AT, j * P:(j + 1) * P].rearrange("p t (r c) -> p t r c", c=QC),
                                q_rows[:, :, :, reversed_columns(j)]).then_inc(queries_gathered, 1)
            dve.wait_ge(bias_landed, 16 * NJ * ROWS * ROWS)
            dve.wait_ge(window_ready, 1 + 2 * NJ * ROWS)
            for j in range(NJ):
                rows = bias[:, j, :, :].rearrange("p h (r k) -> p (h r) k", k=KC)
                link(dve.tensor_tensor(rows, rows, window[:, j, :].unsqueeze(1).broadcast_to([P, NH * ROWS, KC]),
                                       ALU.add))
            flat_prob = prob[:, :, :].rearrange("p h k -> p (h k)")
            for j in range(NJ):
                flat_bias = bias[:, j, :, :].rearrange("p h k -> p (h k)")
                if j > 0:
                    dve.wait_ge(prob_turned, NB * j)
                for g, (s0, s1) in enumerate(SCORE_BANKS):
                    dve.wait_ge(scores_ready, len(SCORE_BANKS) * j + g + 1)
                    dve.scalar_tensor_tensor(flat_prob[:, s0 * NK:s1 * NK], psum[:, g, 0:(s1 - s0) * NK],
                                             HD ** -0.5, flat_bias[:, s0 * NK:s1 * NK], ALU.mult, ALU.add
                                             ).then_inc(scores_read, 1)
                dve.wait_ge(scores_read, len(SCORE_BANKS) * (j + 1))
                link(dve.tensor_reduce(mx[:, :], prob[:, :, :], AX_X, ALU.max))
                dve.tensor_tensor(prob[:, :, :], prob[:, :, :], mx[:, :].unsqueeze(2).broadcast_to([P, NH, NK]),
                                  ALU.subtract).then_inc(centred, 1)
                dve.wait_ge(exp_done, j + 1)
                link(dve.tensor_reduce(den[:, :], prob[:, :, :], AX_X, ALU.add))
                link(dve.reciprocal(rden[:, :], den[:, :]))
                dve.tensor_tensor(prob[:, :, :], prob[:, :, :], rden[:, :].unsqueeze(2).broadcast_to([P, NH, NK]),
                                  ALU.mult).then_inc(prob_ready, 1)

            dve.wait_ge(att_ready, AT * NJ)
            for t in range(LT):
                xin, xc = proj[:, X0 + t, :], proj[:, XC0 + t, :]
                centre = CONV_WIDTH // 2
                link(dve.tensor_scalar(xc, xin, vec(CONV_W + centre * LT + t), vec(CONV_B + t),
                                       ALU.mult, ALU.add))
                for w in (0, 1, 3):
                    d = w - centre
                    o0, o1 = max(0, -d), T - max(0, d)
                    tap = dve.scalar_tensor_tensor(xc[:, o0:o1], xin[:, o0 + d:o1 + d], vec(CONV_W + w * LT + t),
                                                   xc[:, o0:o1], ALU.mult, ALU.add)
                    if w < 3:
                        link(tap)
                    else:
                        tap.then_inc(conv_done, 1)

            for hh in range(2):
                g_tiles = proj[:, G0 + HLT * hh:G0 + HLT * (hh + 1), :].rearrange("p c t -> p (c t)")
                x_tiles = proj[:, X0 + HLT * hh:X0 + HLT * (hh + 1), :]
                xc_tiles = proj[:, XC0 + HLT * hh:XC0 + HLT * (hh + 1), :]
                gelu_tmp = flat(lru_t)[:, 0:HLT * T]
                dve.wait_ge(gelu_sq, hh + 1)
                link(dve.tensor_scalar(gelu_tmp, gelu_tmp, 0.044715, 1.0, ALU.mult, ALU.add))
                dve.tensor_tensor(gelu_tmp, gelu_tmp, g_tiles, ALU.mult).then_inc(gelu_arg, 1)
                dve.wait_ge(gelu_sig, hh + 1)
                dve.tensor_tensor(g_tiles, g_tiles, gelu_tmp, ALU.mult).then_inc(gelu_done, 1)
                dve.wait_ge(conv_done, LT)
                dve.wait_ge(gates_read, 4 * HLT * (hh + 1))
                for z in range(2):
                    link(dve.tensor_tensor(lru_i[:, :, z, :], lru_i[:, :, z, :], xc_tiles, ALU.mult))
                dve.wait_ge(decay_done, 2 * HLT * (hh + 1))
                dve.wait_ge(sqrt_done, hh + 1)
                link(dve.scalar_tensor_tensor(flat(lru_s), flat(lru_r), 1.0, flat(lru_s), ALU.add, ALU.mult))
                link(dve.tensor_tensor(flat(lru_i), flat(lru_s), flat(lru_i), ALU.mult))
                link(dve.scalar_tensor_tensor(flat(lru_t), flat(lru_r), 1.0, flat(lru_t), ALU.add, ALU.mult))
                link(dve.tensor_scalar(flat(lru_r), flat(lru_t), -1.0, 1.0, ALU.mult, ALU.add))
                for c in range(HLT):
                    dve.tensor_tensor_scan(lru_s[:, c, 0, :], lru_r[:, c, 0, :], lru_i[:, c, 0, :], 0.0,
                                           ALU.mult, ALU.add).then_inc(scanned, 1)
                    dve.tensor_tensor_scan(lru_s[:, c, 1, ::-1], lru_r[:, c, 1, ::-1], lru_i[:, c, 1, ::-1], 0.0,
                                           ALU.mult, ALU.add).then_inc(scanned, 1)
                dve.wait_ge(scanned, 2 * HLT * (hh + 1))
                link(dve.tensor_tensor(x_tiles, lru_s[:, :, 0, :], lru_s[:, :, 1, :], ALU.add))
                dve.wait_ge(gelu_done, hh + 1)
                flat_x = x_tiles.rearrange("p c t -> p (c t)")
                dve.tensor_tensor(flat_x, flat_x, g_tiles, ALU.mult).then_inc(lru_done, 1)

            for n, (t0, e_base, v_base, gain) in enumerate(((X0, E_LRU, V_LRU, G_LRU), (Q0, E_ATT, V_ATT, G_ATT))):
                for t in range(0, LT, CT):
                    sum_squares(e_base + t)
                norm(N_LRU + n, proj[:, t0:t0 + LT, :], gain, v_base, LT)
            splits(C_MIX_OUT, 2, 4)
            with dve.Fori(0, 2) as i:
                down(C_MIX_OUT, M_MIX_OUT, H_MIX, E_MIX, 2 * DT, G_FFN2, UP_KS, 1.0, i)
            scales(N_FFN2)
            with dve.Fori(0, UP_BLOCKS) as i:
                hidden(C_UP2, M_UP2, FT, i)
            down(C_DOWN2, M_DOWN2, H_DOWN2, E_DOWN2, 0, None, DOWN_KS, 0.5, 0)
            down(C_DOWN2, M_DOWN2, H_DOWN2, E_DOWN2, 0, None, DOWN_KS, 0.5, 1, final=True)
            dve.wait_ge(std_ready, N_FINAL + 1)
            link(dve.reciprocal(rstd[:, 0:2], std[:, 0:2]))
            for half in range(2):
                for g in range(4):
                    dve.wait_ge(fin_turned, 4 * half + g + 1)
                    dve.tensor_scalar(fin_nat[:, half, 512 * g:512 * (g + 1)], psum[:, 4 * half + g, :],
                                      rstd[:, half:half + 1], None, ALU.mult).then_inc(fin_out, 1)


_INS = ['x', 'norm_ffn1', 'ffn1_w_in', 'ffn1_w_out', 'norm_mix', 'w_in_mix', 'lru_conv_w', 'lru_conv_b',
        'lru_gate_w', 'lru_gate_b', 'lru_lambda', 'attn_rpb', 'lru_out_norm', 'attn_out_norm', 'w_out_mix',
        'norm_ffn2', 'ffn2_w_in', 'ffn2_w_out', 'norm_final']
_OUTS = [((1, 256, 2048), 'float32')]


def kernel(**inputs):
    import numpy as _np
    import concourse.bacc as _bacc
    from concourse import mybir as _mybir
    from concourse.bass_utils import run_bass_kernel_spmd as _run

    nc = _bacc.Bacc("TRN2", target_bir_lowering=False, num_devices=1)
    arrays, args = {}, []
    for name in _INS:
        a = _np.ascontiguousarray(inputs[name])
        arrays[f"in_{name}_dram"] = a
        args.append(nc.dram_tensor(f"in_{name}_dram", a.shape, _mybir.dt.from_np(a.dtype), kind="ExternalInput").ap())
    for i, (shape, dtype) in enumerate(_OUTS):
        dt = _mybir.dt.from_np(_np.dtype(dtype))
        args.append(nc.dram_tensor(f"out_{i}_dram", shape, dt, kind="ExternalOutput").ap())
    hybrid_encoder_block(nc, *args)
    r = _run(nc, [arrays], core_ids=[0])
    got = tuple(r.results[0][f"out_{i}_dram"] for i in range(len(_OUTS)))
    return got[0]
```

```python
import math
from contextlib import ExitStack

import concourse.bass as bass
from concourse import mybir

P = 128
F32 = mybir.dt.float32
F32R = mybir.dt.float32r
ALU = mybir.AluOpType
ACT = mybir.ActivationFunctionType
AX_X = mybir.AxisListType.X
RADD = bass.bass_isa.ReduceOp.add

GRID_W = 64
WIN_ROWS = 8
WIN_COLS = 16
CONV_WIDTH = 4
EPS = 1e-6
RG_C = 8.0
MASKED = -1e30


def hybrid_encoder_block(
    nc: bass.Bass,
    x: bass.AP,
    norm_ffn1: bass.AP,
    ffn1_w_in: bass.AP,
    ffn1_w_out: bass.AP,
    norm_mix: bass.AP,
    w_in_mix: bass.AP,
    lru_conv_w: bass.AP,
    lru_conv_b: bass.AP,
    lru_gate_w: bass.AP,
    lru_gate_b: bass.AP,
    lru_lambda: bass.AP,
    attn_rpb: bass.AP,
    lru_out_norm: bass.AP,
    attn_out_norm: bass.AP,
    w_out_mix: bass.AP,
    norm_ffn2: bass.AP,
    ffn2_w_in: bass.AP,
    ffn2_w_out: bass.AP,
    norm_final: bass.AP,
    out: bass.AP,
):
    _, T, D = x.shape
    F = ffn1_w_out.shape[1]
    L = lru_conv_w.shape[2]
    A = w_in_mix.shape[2] // 3 - 2 * L // 3
    NH, _, NDC = attn_rpb.shape[1:]
    HD = A // NH
    DT, FT, LT, AT = D // P, F // P, L // P, A // P
    ROWS = T // GRID_W
    assert T == 256 and D == 2048 and L == A == D // 2 and HD == 64 and F % 512 == 0 and ROWS == 4

    CK, CN = 4, 512
    CT = CN // P
    RING = 4
    UP_BLOCKS = F // CN
    UP_KS = DT // CK
    DOWN_KS = FT // CK
    MIX_GROUPS = (2 * L + 3 * A) // CN
    OUT_GROUPS = D // CN
    C_UP1 = 0
    C_DOWN1 = C_UP1 + UP_BLOCKS * 2 * UP_KS
    C_MIX_IN = C_DOWN1 + D // CN * DOWN_KS
    C_MIX_OUT = C_MIX_IN + MIX_GROUPS * UP_KS
    C_UP2 = C_MIX_OUT + D // CN * UP_KS
    C_DOWN2 = C_UP2 + (C_DOWN1 - C_UP1)
    NB = 8
    M_UP1 = NB
    M_DOWN1 = M_UP1 + UP_BLOCKS * 2 * CT
    M_MIX_IN = M_DOWN1 + DT
    M_MIX_OUT = M_MIX_IN + MIX_GROUPS * CT
    M_UP2 = M_MIX_OUT + 2 * DT
    M_DOWN2 = M_UP2 + UP_BLOCKS * 2 * CT
    E_X, E_DOWN1, E_LRU, E_ATT = 0, DT, 2 * DT, 2 * DT + LT
    E_MIX, E_DOWN2, E_END = 3 * DT, 4 * DT, 5 * DT
    H_DOWN1, H_LRU, H_ATT, H_DOWN2 = 0, DT, 2 * DT, 3 * DT
    V_FFN1, V_MIX, V_LRU, V_ATT, V_FFN2 = 0, DT, 2 * DT, 2 * DT + LT, 3 * DT
    N_FFN1, N_MIX, N_LRU, N_ATT, N_FFN2, N_FINAL = range(6)
    X0, G0, Q0, K0, V0 = 0, LT, 2 * LT, 2 * LT + AT, 2 * LT + 2 * AT
    XC0 = V0
    S_OUT = MIX_GROUPS * UP_KS
    HALF_KS = UP_KS // 2
    S_END = S_OUT + 2 * OUT_GROUPS * HALF_KS
    UT = 2
    UNITS = LT // UT
    HLT = LT // 2

    QC = P // ROWS
    NJ = GRID_W // QC
    KS0 = 24
    KC = 40
    KR2 = 2 * KC
    NK = ROWS * KC
    HALF_WIN = WIN_COLS // 2
    HPB = 512 // NK
    HEAD_SLOT = [(head % 2) * (NH // 2) + head // 2 for head in range(NH)]
    SCORE_BANKS = [(par * (NH // 2) + a, par * (NH // 2) + min(a + HPB, NH // 2))
                   for par in range(2) for a in range(0, NH // 2, HPB)]
    DR0 = WIN_ROWS - ROWS
    NDRU = 2 * ROWS - 1
    PAD = 24
    PADW = 80

    ctx = ExitStack()
    with ctx:
        def sem(name):
            return ctx.enter_context(nc.semaphore(name))

        def sb(name, shape, dt=F32, stack=ctx):
            return stack.enter_context(nc.sbuf_tensor(name, shape, dt))

        rpb_padded = nc.dram_tensor("rpb_padded", [NH, NDRU, PADW], F32, kind="Internal").ap()

        psum = ctx.enter_context(nc.psum_tensor("psum", [P, NB, 512], F32))

        h = sb("h", [P, DT, T])
        w_hi = [sb(f"w_hi{s}", [P, CK, CN], F32R) for s in range(2)]
        w_raw, w_lo = [], []
        for s in range(RING):
            with ExitStack() as region:
                w_raw.append(sb(f"w_raw{s}", [P, CK, CN], F32, region))
            w_lo.append(sb(f"w_lo{s}", [P, CK, CN], F32R))
        half_b = sb("half_b", [P, CT, T])
        gbuf = sb("gbuf", [P, CT, T])
        ubuf = sb("ubuf", [P, CT, T])
        sumsq = sb("sumsq", [P, T])
        stat = sb("stat", [P, T])
        std = sb("std", [P, T])
        rstd = sb("rstd", [P, T])
        mix_rstd = sb("mix_rstd", [P, T])
        ident = sb("ident", [P, P])
        ones = sb("ones", [P, P])
        eps = sb("eps", [P, 1])
        vec_rows = [sb(f"vec_rows{s}", [P, P]) for s in range(2)]
        vecs = sb("vecs", [P, 2 * P])
        lam_exp = sb("lam_exp", [P, 2 * LT])
        sp_s = sb("sp_s", [P, 2 * LT])
        sp_s2 = sb("sp_s2", [P, 2 * LT])
        sp_q = sb("sp_q", [P, 2 * LT])
        decay4 = sb("decay4", [P, 2 * LT])
        decay8n = sb("decay8n", [P, 2 * LT])
        mx = sb("mx", [P, NH])
        den = sb("den", [P, NH])
        rden = sb("rden", [P, NH])
        window = sb("window", [P, NJ, KC])

        with ExitStack() as region:
            act_t = sb("act_t", [P, DT, 2, T], F32R, region)
        with ExitStack() as region:
            v_nat = sb("v_nat", [KR2, NJ, 2, A], F32, region)
            p_t = sb("p_t", [KR2, NH, 2, P], F32, region)
        with ExitStack() as region:
            fin_t = sb("fin_t", [P, DT, T], F32, region)
            fin_nat = sb("fin_nat", [P, 2, D], F32, region)
        sb("region_u", [P, DT, 2, T])
        with ExitStack() as region:
            hid_t = sb("hid_t", [P, FT, 2, T], F32R, region)
        with ExitStack() as region:
            x_nat = sb("x_nat", [P, 2, D], F32, region)
        with ExitStack() as region:
            proj = sb("proj", [P, 2 * LT + 3 * AT, T], F32, region)
            with ExitStack() as inner:
                lru_r, lru_i, lru_t, lru_s = [], [], [], []
                for k in range(2):
                    for name, bufs in (("r", lru_r), ("i", lru_i), ("t", lru_t), ("s", lru_s)):
                        bufs.append(sb(f"lru_{name}{k}", [P, UT, 2, T], F32, inner))
                gate_w = sb("gate_w", [P, LT, 4, P], F32, inner)
            with ExitStack() as inner:
                bias = sb("bias", [P, NJ, NH, NK], F32, inner)
                prob = sb("prob", [P, NJ, NH, NK], F32, inner)
                queries_t = sb("queries_t", [P, AT, NJ, P], F32, inner)
            with ExitStack() as inner:
                v_keys = sb("v_keys", [P, NJ, 2, AT, KR2], F32, inner)
        with ExitStack() as region:
            mix_t = sb("mix_t", [P, 2, 2, LT, T], F32R, region)
        sb("region_h", [P, FT, 2, T])

        raw_landed = [sem(f"raw_landed{s}") for s in range(RING)]
        hi_split = sem("hi_split")
        lo_split = sem("lo_split")
        columns_done = sem("columns_done")
        half_copied = sem("half_copied")
        bank_free = sem("bank_free")
        gate_scaled = sem("gate_scaled")
        up_scaled = sem("up_scaled")
        silu_done = sem("silu_done")
        act_hi = sem("act_hi")
        proj_scaled = sem("proj_scaled")
        hidden_full = sem("hidden_full")
        hidden_hi = sem("hidden_hi")
        hidden_ready = sem("hidden_ready")
        h_written = sem("h_written")
        squared = sem("squared")
        squares_added = sem("squares_added")
        sumsq_clear = sem("sumsq_clear")
        sumsq_done = sem("sumsq_done")
        stat_ready = sem("stat_ready")
        std_ready = sem("std_ready")
        rstd_ready = sem("rstd_ready")
        normed_full = sem("normed_full")
        normed_hi = sem("normed_hi")
        act_ready = sem("act_ready")
        x_landed = [[sem(f"x_landed{half}_{q}") for q in range(4)] for half in range(2)]
        x_turned = sem("x_turned")
        consts = sem("consts")
        vec_clear = sem("vec_clear")
        vec_landed = sem("vec_landed")
        late_vec_landed = sem("late_vec_landed")
        table_in = sem("table_in")
        vec_turned = sem("vec_turned")
        vecs_ready = sem("vecs_ready")
        lam_exp_done = sem("lam_exp_done")
        decay_ready = sem("decay_ready")
        chain = sem("chain")
        pad_zero = sem("pad_zero")
        pad_done = sem("pad_done")
        bias_landed = [sem(f"bias_landed{j}") for j in range(NJ)]
        gate_zero = sem("gate_zero")
        gate_landed = sem("gate_landed")
        window_ready = sem("window_ready")
        keys_gathered = sem("keys_gathered")
        queries_gathered = sem("queries_gathered")
        v_turned = sem("v_turned")
        v_ready = sem("v_ready")
        scores_ready = sem("scores_ready")
        scores_read = sem("scores_read")
        centred = sem("centred")
        exp_done = sem("exp_done")
        prob_ready = sem("prob_ready")
        prob_turned = sem("prob_turned")
        prob_t_ready = sem("prob_t_ready")
        att_ready = sem("att_ready")
        att_read = sem("att_read")
        conv_done = sem("conv_done")
        gates_ready = sem("gates_ready")
        gates_read = sem("gates_read")
        centre_done = sem("centre_done")
        scaled_one = sem("scaled_one")
        complement_done = sem("complement_done")
        summed = sem("summed")
        bias_ready = sem("bias_ready")
        tanh_done = sem("tanh_done")
        decay_done = sem("decay_done")
        sqrt_done = sem("sqrt_done")
        gelu_sq = sem("gelu_sq")
        gelu_arg = sem("gelu_arg")
        gelu_sig = sem("gelu_sig")
        gelu_done = sem("gelu_done")
        scanned = sem("scanned")
        lru_done = sem("lru_done")
        fin_scaled = sem("fin_scaled")
        fin_turned = sem("fin_turned")
        fin_even = sem("fin_even")
        fin_odd = sem("fin_odd")
        out_written = sem("out_written")

        up1 = ffn1_w_in[0].rearrange("(t p) n -> p t n", p=P)
        up2 = ffn2_w_in[0].rearrange("(t p) n -> p t n", p=P)
        down1 = ffn1_w_out[0].rearrange("(t p) n -> p t n", p=P)
        down2 = ffn2_w_out[0].rearrange("(t p) n -> p t n", p=P)
        mix_in = w_in_mix[0].rearrange("(t p) n -> p t n", p=P)
        mix_out = w_out_mix[0].rearrange("(t p) n -> p t n", p=P)

        vec_parts = [[(norm_ffn1[0], DT), (norm_mix[0], DT), (norm_ffn2[0], DT), (norm_final, DT),
                      (lru_out_norm[0], LT), (attn_out_norm[0], AT), (lru_conv_b[0], LT)],
                     [(lru_conv_w[0].rearrange("w c -> (w c)"), CONV_WIDTH * LT),
                      (lru_gate_b[0].rearrange("z g h d -> (z g h d)"), 4 * LT),
                      (lru_lambda[0].rearrange("z c -> (z c)"), 2 * LT)]]
        vec_parts = [[(values, n, s, sum(m for _, m in parts[:k])) for k, (values, n) in enumerate(parts)]
                     for s, parts in enumerate(vec_parts)]

        def load_vector(engine, part, landed):
            values, n, s, at = part
            engine.dma_start(vec_rows[s][at:at + n, :], values.rearrange("(t p) -> t p", p=P)
                             ).then_inc(landed, 16)

        G_FFN1, G_MIX, G_FFN2, G_FINAL = 0, DT, 2 * DT, 3 * DT
        G_LRU, G_ATT, CONV_B = 4 * DT, 4 * DT + LT, 4 * DT + LT + AT
        CONV_W, GATE_B, LAMBDA = P, P + CONV_WIDTH * LT, P + (CONV_WIDTH + 4) * LT

        def vec(column):
            return vecs[:, bass.ds(column, 1)]

        def grid(tile):
            return tile.rearrange("p (r c) -> p r c", c=GRID_W)

        mixed = [mix_t[:, part].rearrange("p s k t -> p k s t") for part in range(2)]

        def mix_chunk(s):
            if s < S_OUT:
                return s // UP_KS, s % UP_KS, UP_KS
            return MIX_GROUPS + (s - S_OUT) // HALF_KS, (s - S_OUT) % HALF_KS, HALF_KS

        def ends_group(s):
            group, ks, n_ks = mix_chunk(s)
            return s < S_END and ks == n_ks - 1

        def first_bank(group):
            return CT * (group % 2) if group >= MIX_GROUPS + OUT_GROUPS else 0

        def reversed_columns(j):
            return slice((j + 1) * QC - 1, j * QC - 1 if j else None, -1)

        first_squares = [buf[:, :, :].rearrange("p c t -> p (c t)") for buf in (gbuf, ubuf, half_b, ubuf)]

        def h4(q):
            return h[:, CT * q:CT * (q + 1), :].rearrange("p c t -> p (c t)")

        def flat(buf):
            return buf[:, :, :, :].rearrange("p c z t -> p (c z t)")

        gelu_tmp = [buf[:, :, :].rearrange("p c t -> p (c t)") for buf in (gbuf, ubuf)]

        def g_half(hh):
            return proj[:, G0 + HLT * hh:G0 + HLT * (hh + 1), :].rearrange("p c t -> p (c t)")


        block = ctx.enter_context(nc.Block())

        @block.sync
        def _(sp):
            sp.wait_ge(vec_clear, 2)
            for part in vec_parts[1][1:]:
                load_vector(sp, part, late_vec_landed)
            for q in range(4):
                for half in range(2):
                    cols = slice(q * D // 4, (q + 1) * D // 4)
                    sp.dma_start(x_nat[:, half, cols], x[0, half * P:(half + 1) * P, cols]
                                 ).then_inc(x_landed[half][q], 16)

            def load(weights, n, j, ks, column, fill=False):
                if not fill:
                    sp.wait_ge(columns_done, CT * (n - RING + 1))
                sp.dma_start(w_raw[j % RING][:, :, :],
                             weights[:, CK * ks:CK * (ks + 1), bass.ds(column, CN)]
                             ).then_inc(raw_landed[j % RING], 16)

            def two_columns(weights, base, i, column, apart, fill=False):
                for ks in range(UP_KS):
                    for side in range(2):
                        j = 2 * ks + side
                        load(weights, base + 2 * UP_KS * i + j, j, ks, column + side * apart,
                             fill=fill and j < RING)

            def groups(weights, base, n_ks, ks0=0, g0=0, count=OUT_GROUPS):
                for group in range(count):
                    for ks in range(n_ks):
                        j = n_ks * group + ks
                        load(weights, base + j, j, ks0 + ks, (g0 + group) * CN)

            two_columns(up1, C_UP1, 0, 0, F, fill=True)
            with sp.Fori(1, UP_BLOCKS) as i:
                two_columns(up1, C_UP1, i, i * CN, F)
            groups(down1, C_DOWN1, DOWN_KS)
            groups(mix_in, C_MIX_IN, UP_KS, count=1)
            sp.wait_ge(gate_zero, 1)
            for zg in range(4):
                source = lru_gate_w[0, zg // 2, zg % 2].rearrange("(t two) i j -> two i t j", two=2)
                for par in range(2):
                    part = slice(HD * par, HD * (par + 1))
                    sp.dma_start(gate_w[part, :, zg, part], source[par]).then_inc(gate_landed, 16)
            with sp.Fori(1, MIX_GROUPS) as i:
                groups(mix_in, C_MIX_IN + UP_KS * i, UP_KS, g0=i, count=1)
            for part in range(2):
                groups(mix_out, C_MIX_OUT + OUT_GROUPS * HALF_KS * part, HALF_KS, ks0=HALF_KS * part)
            with sp.Fori(0, UP_BLOCKS) as i:
                two_columns(up2, C_UP2, i, i * CN, F)
            groups(down2, C_DOWN2, DOWN_KS)
            for half in range(2):
                for g in range(4):
                    sp.wait_ge((fin_even, fin_odd)[g % 2], 2 * half + g // 2 + 1)
                    sp.dma_start(out[0, half * P:(half + 1) * P, 512 * g:512 * (g + 1)],
                                 fin_nat[:, half, 512 * g:512 * (g + 1)]).then_inc(out_written, 16)
            sp.wait_ge(out_written, 16 * 8)

        @block.gpsimd
        def _(pool):
            pool.memset(ident[:, :], 0.0).then_inc(consts, 1)
            pool.memset(ones[:, :], 1.0).then_inc(consts, 1)
            pool.wait_ge(consts, 2)
            pool.affine_select(out=ident[:, :], in_=ident[:, :], compare_op=ALU.not_equal, fill=1.0,
                               base=0, pattern=[[-1, P]], channel_multiplier=1).then_inc(consts, 1)
            pool.wait_ge(consts, 3)
            pool.memset(window[:, :, :], 0.0).then_inc(window_ready, 1)
            done = 1
            for j in range(NJ):
                low = min(KC, GRID_W - WIN_COLS - j * KS0)
                high = max(0, WIN_COLS - j * KS0)
                shift = j * (KS0 - QC)
                for r in range(ROWS):
                    row = window[r * QC:(r + 1) * QC, j, :]
                    pool.wait_ge(window_ready, done)
                    pool.affine_select(out=row[:, 0:low], in_=row[:, 0:low], compare_op=ALU.is_ge,
                                       fill=MASKED, base=shift + HALF_WIN - (QC - 1),
                                       pattern=[[1, low]], channel_multiplier=1).then_inc(window_ready, 1)
                    done += 1
                    pool.wait_ge(window_ready, done)
                    pool.affine_select(out=row[:, high:KC], in_=row[:, high:KC], compare_op=ALU.is_ge,
                                       fill=MASKED, base=HALF_WIN - 1 - shift - high + QC - 1,
                                       pattern=[[-1, KC - high]], channel_multiplier=-1).then_inc(window_ready, 1)
                    done += 1

            def square_sum(n, e_end):
                pool.wait_ge(sumsq_done, e_end)
                pool.partition_all_reduce(stat[:, :], sumsq[:, :], P, RADD).then_inc(stat_ready, 1)
                pool.wait_ge(stat_ready, n + 1)

            pool.wait_ge(vecs_ready, 1)
            pool.wait_ge(window_ready, done)
            pool.memset(vec_rows[0][:, :], 0.0).then_inc(pad_zero, 1)
            pool.wait_ge(pad_zero, 1)
            pool.dma_start(rpb_padded.rearrange("h r w -> (h r) w"), vec_rows[0][0:NH * NDRU, 0:PADW]
                           ).then_inc(pad_done, 16)
            pool.wait_ge(pad_done, 16)
            for par in range(2):
                heads = attn_rpb[0, :, DR0:DR0 + NDRU, :].rearrange("(t two) r c -> two t r c", two=2)[par]
                pool.dma_start(rpb_padded[par * (NH // 2):(par + 1) * (NH // 2), :, PAD:PAD + NDC], heads
                               ).then_inc(pad_done, 16)
            pool.wait_ge(pad_done, 48)
            square_sum(N_FFN1, E_X + DT)
            pool.wait_ge(columns_done, CT * C_MIX_IN)
            pool.memset(gate_w[:, :, :, :], 0.0).then_inc(gate_zero, 1)
            pool.wait_ge(gate_zero, 1)
            square_sum(N_MIX, E_DOWN1 + DT)
            pool.wait_ge(proj_scaled, Q0 + AT)
            pool.wait_ge(gates_ready, LT)
            q_rows = proj[:, Q0:Q0 + AT, :].rearrange("p t (r c) -> p t r c", c=GRID_W)
            for j in range(NJ):
                pool.tensor_copy(queries_t[:, :, j, :].rearrange("p t (r c) -> p t r c", c=QC),
                                 q_rows[:, :, :, reversed_columns(j)]).then_inc(queries_gathered, 1)
                pool.wait_ge(queries_gathered, j + 1)
            for j in range(NJ):
                pool.wait_ge(summed, UNITS - 1 + j)
                for r in range(ROWS):
                    for kr in range(ROWS):
                        start = (kr - r + ROWS - 1) * PADW + PAD + WIN_COLS - QC + j * (KS0 - QC)
                        sheared = bass.AP(rpb_padded.tensor, start, [[1, QC], [NDRU * PADW, NH], [1, KC]])
                        pool.dma_start(bias[r * QC:(r + 1) * QC, j, :, kr * KC:(kr + 1) * KC], sheared
                                       ).then_inc(bias_landed[j], 16)
                if j == 0:
                    square_sum(N_LRU, E_LRU + LT)
                pool.wait_ge(bias_landed[j], 16 * ROWS * ROWS)
                rows = bias[:, j, :, :].rearrange("p h (r k) -> p (h r) k", k=KC)
                pool.tensor_tensor(rows, rows, window[:, j, :].unsqueeze(1).broadcast_to([P, NH * ROWS, KC]),
                                   ALU.add).then_inc(bias_ready, 1)
                pool.wait_ge(bias_ready, j + 1)
            square_sum(N_ATT, E_ATT + AT)
            square_sum(N_FFN2, E_MIX + DT)

        @block.tensor
        def _(pe):
            def chunk(n, j, rhs, k0, m, b0, first, last, banks=NB):
                pe.wait_ge(lo_split, n + 1)
                for c in range(CT):
                    if first:
                        pe.wait_ge(bank_free, m + c - (banks - 1))
                    both = psum[:, b0 + c, :].rearrange("p (s t) -> p s t", t=T)
                    for k in range(CK):
                        hi = w_hi[j % 2][:, k, c * P:(c + 1) * P]
                        lo = w_lo[j % RING][:, k, c * P:(c + 1) * P]
                        a_both = rhs[:, k0 + k, :, :]
                        a_hi = rhs[:, k0 + k, 0, :]
                        if last and k == CK - 1:
                            pe.matmul(psum[:, b0 + c, 0:T], lo, a_hi, start=False, stop=False)
                            mm = pe.matmul(both, hi, a_both, start=False, stop=True)
                        else:
                            pe.matmul(both, hi, a_both, start=first and k == 0, stop=False)
                            mm = pe.matmul(psum[:, b0 + c, 0:T], lo, a_hi, start=False, stop=False)
                    mm.then_inc(columns_done, 1)

            def two_columns(c_base, m_base, v_base, i):
                for ks in range(UP_KS):
                    pe.wait_ge(act_ready, v_base + CK * (ks + 1))
                    for side in range(2):
                        j = 2 * ks + side
                        chunk(c_base + 2 * UP_KS * i + j, j, act_t, CK * ks,
                              m_base + 2 * CT * i + CT * side, CT * side, ks == 0, ks == UP_KS - 1)

            def down(c_base, m_base, n_ks, rhs, ready, ready_base):
                for group in range(OUT_GROUPS):
                    for ks in range(n_ks):
                        pe.wait_ge(ready, ready_base + CK * (ks + 1))
                        j = n_ks * group + ks
                        chunk(c_base + j, j, rhs, CK * ks, m_base + CT * group, CT * (group % 2),
                              ks == 0, ks == n_ks - 1)

            pe.wait_ge(consts, 3)
            for t in range(DT):
                if t % 4 == 0:
                    for half in range(2):
                        pe.wait_ge(x_landed[half][t // 4], 16)
                if t == DT - 2:
                    pe.wait_ge(vec_landed, 16 * (len(vec_parts[0]) + 1))
                    pe.wait_ge(late_vec_landed, 16 * (len(vec_parts[1]) - 1))
                    for s in range(2):
                        mm = pe.transpose(psum[:, NB - 1, s * P:(s + 1) * P], vec_rows[s][:, :], ident[:, :])
                    mm.then_inc(vec_turned, 1)
                    pe.wait_ge(vecs_ready, 1)
                for half in range(2):
                    mm = pe.transpose(psum[:, t // 2, (t % 2) * T + half * P:(t % 2) * T + (half + 1) * P],
                                      x_nat[:, half, t * P:(t + 1) * P], ident[:, :])
                if t % 2 == 1:
                    mm.then_inc(x_turned, 1)

            with pe.Fori(0, UP_BLOCKS) as i:
                two_columns(C_UP1, M_UP1, V_FFN1, i)
            down(C_DOWN1, M_DOWN1, DOWN_KS, hid_t, hidden_ready, 0)

            def steps(s0, s1):
                for s in range(s0, s1):
                    group, ks, n_ks = mix_chunk(s)
                    if s < S_OUT:
                        rhs, ready = act_t, V_MIX
                    else:
                        part = (group - MIX_GROUPS) // OUT_GROUPS
                        rhs, ready = mixed[part], V_LRU + LT * part
                    pe.wait_ge(act_ready, ready + CK * (ks + 1))
                    few = 1 <= group <= MIX_GROUPS + OUT_GROUPS
                    chunk(C_MIX_IN + s, s, rhs, CK * ks, M_MIX_IN + CT * group, first_bank(group),
                          ks == 0, ks == n_ks - 1, banks=CT if few else NB)

            def gates(u):
                if u > 0:
                    pe.wait_ge(gates_read, 4 * UT * u)
                for c in range(UT):
                    t = UT * u + c
                    pe.wait_ge(conv_done, t + 1)
                    for zg in range(4):
                        mm = pe.matmul(psum[:, CT + 2 * c + zg // 2, (zg % 2) * T:(zg % 2 + 1) * T],
                                       gate_w[:, t, zg, :], proj[:, XC0 + t, :], start=True, stop=True)
                    mm.then_inc(gates_ready, 1)

            def scores(n0, n1):
                for n in range(n0, n1):
                    j, g = divmod(n, len(SCORE_BANKS))
                    s0, s1 = SCORE_BANKS[g]
                    if n >= CT:
                        pe.wait_ge(scores_read, n - CT + 1)
                    for slot in range(s0, s1):
                        par, tile = divmod(slot, NH // 2)
                        part = slice(HD * par, HD * (par + 1))
                        keys = grid(proj[part, K0 + tile, :])[:, :, j * KS0:j * KS0 + KC]
                        mm = pe.matmul(psum[:, CT + n % CT, (slot - s0) * NK:(slot - s0 + 1) * NK],
                                       queries_t[part, tile, j, :], keys, start=True, stop=True)
                    mm.then_inc(scores_ready, 1)

            def turn_probs(j, pair0, pair1):
                for pair in range(pair0, pair1):
                    if pair >= CT:
                        pe.wait_ge(prob_t_ready, NB * j + pair - CT + 1)
                    for head in (2 * pair, 2 * pair + 1):
                        for m in range(2):
                            col = ((head % 2) * 2 + m) * P
                            mm = pe.transpose(psum[0:KR2, CT + pair % CT, col:col + P],
                                              prob[:, j, HEAD_SLOT[head], m * KR2:(m + 1) * KR2], ident[:, :])
                    mm.then_inc(prob_turned, 1)

            def turn_values(g0, g1):
                for g in range(g0, g1):
                    j, m, half = g // 4, (g // 2) % 2, g % 2
                    if g >= CT:
                        pe.wait_ge(v_ready, g - CT + 1)
                    pe.wait_ge(keys_gathered, 2 * j + m + 1)
                    for t in range(4):
                        mm = pe.transpose(psum[0:KR2, CT + g % CT, t * P:(t + 1) * P],
                                          v_keys[:, j, m, 4 * half + t, :], ident[:, :])
                    mm.then_inc(v_turned, 1)

            def attend(j):
                pe.wait_ge(prob_t_ready, NB * (j + 1))
                pe.wait_ge(v_ready, NB)
                for head in range(NH):
                    part = slice(HD * (head % 2), HD * (head % 2 + 1))
                    pair = head // 2
                    for m in range(2):
                        mm = pe.matmul(psum[part, CT + pair // 4, (pair % 4) * P:(pair % 4 + 1) * P],
                                       v_nat[:, j, m, head * HD:(head + 1) * HD], p_t[:, head, m, :],
                                       start=(m == 0), stop=(m == 1))
                    if head % 2 == 1:
                        mm.then_inc(att_ready, 1)

            steps(0, 5)
            pe.wait_ge(gate_landed, 16 * 8)
            gates(0)
            steps(5, 10)
            gates(1)
            steps(10, 15)
            gates(2)
            steps(15, 20)
            gates(3)
            steps(20, 33)
            pe.wait_ge(queries_gathered, NJ)
            pe.wait_ge(proj_scaled, K0 + AT)
            pe.wait_ge(gates_read, 4 * LT)
            scores(0, 4)
            steps(33, 34)
            scores(4, 6)
            steps(34, 35)
            scores(6, 8)
            steps(35, 36)
            scores(8, 10)
            steps(36, 38)
            scores(10, 12)
            steps(38, 40)
            pe.wait_ge(prob_ready, 1)
            pe.wait_ge(scores_read, NJ * len(SCORE_BANKS))
            turn_probs(0, 0, 4)
            steps(40, 41)
            turn_probs(0, 4, 8)
            steps(41, 42)
            pe.wait_ge(prob_t_ready, NB)
            turn_values(0, 4)
            steps(42, 43)
            turn_values(4, 8)
            steps(43, 44)
            attend(0)
            steps(44, 45)
            pe.wait_ge(prob_ready, 2)
            pe.wait_ge(att_read, AT)
            turn_probs(1, 0, 4)
            steps(45, 46)
            turn_probs(1, 4, 8)
            steps(46, 47)
            attend(1)
            steps(47, S_END)

            with pe.Fori(0, UP_BLOCKS) as i:
                two_columns(C_UP2, M_UP2, V_FFN2, i)
            down(C_DOWN2, M_DOWN2, DOWN_KS, hid_t, hidden_ready, FT)

            def turn_out(half, t0, t1):
                for t in range(t0, t1):
                    if half == 0:
                        pe.wait_ge(fin_scaled, t + 1)
                    mm = pe.transpose(psum[:, 4 * half + t // 4, (t % 4) * P:(t % 4 + 1) * P],
                                      fin_t[:, t, half * P:(half + 1) * P], ident[:, :])
                    if t % 4 == 3:
                        mm.then_inc(fin_turned, 1)

            turn_out(0, 0, DT)
            pe.wait_ge(sumsq_done, E_END - CT)
            pe.wait_ge(squared, E_END)
            for side in range(2):
                tokens = slice(side * P, (side + 1) * P)
                total = psum[:, NB - 1, side:side + 1]
                pe.matmul(total, sumsq[:, tokens], ones[:, 0:1], start=True, stop=False)
                for c in range(CT):
                    mm = pe.matmul(total, gbuf[:, c, tokens], ones[:, 0:1], start=False, stop=c == CT - 1)
            mm.then_inc(stat_ready, 1)
            turn_out(1, 0, DT - 4)
            pe.wait_ge(std_ready, N_FINAL + 1)
            turn_out(1, DT - 4, DT)

        @block.scalar
        def _(act):
            def splits(n0, j0, j1, fill=False):
                for j in range(j0, j1):
                    act.wait_ge(raw_landed[j % RING], 16 * (j // RING + 1) + n0 * (16 // RING))
                    if not fill:
                        act.wait_ge(columns_done, CT * (n0 + j - 1))
                    act.copy(w_hi[j % 2][:, :, :], w_raw[j % RING][:, :, :]).then_inc(hi_split, 1)

            def copy_halves(n, m, b0):
                for c in range(CT):
                    act.wait_ge(columns_done, CT * n + c + 1)
                    act.wait_ge(bank_free, m + c - (CT - 1))
                    act.copy(half_b[:, c, :], psum[:, b0 + c, T:2 * T]).then_inc(half_copied, 1)

            def hidden(c_base, m_base, f_base, i, j0=4):
                n0 = c_base + 2 * UP_KS * i
                m = m_base + 2 * CT * i
                splits(n0, j0, 8)
                copy_halves(n0 + 2 * UP_KS - 2, m, 0)
                splits(n0, 8, 9)
                copy_halves(n0 + 2 * UP_KS - 1, m + CT, CT)
                splits(n0, 9, 10)
                for c in range(CT):
                    act.wait_ge(gate_scaled, f_base + CT * i + c + 1)
                    act.activation(gbuf[:, c, :], gbuf[:, c, :], ACT.Silu).then_inc(silu_done, 1)
                splits(n0, 10, 11)
                for c in range(CT):
                    act.wait_ge(hidden_full, f_base + CT * i + c + 1)
                    act.copy(hid_t[:, CT * i + c, 0, :], ubuf[:, c, :]).then_inc(hidden_hi, 1)
                splits(n0, 11, 12)

            def high(t, gain, ready, count):
                act.wait_ge(ready, count)
                act.activation(act_t[:, t, 0, :], h[:, t, :], ACT.Copy, scale=vec(gain + t)).then_inc(act_hi, 1)

            def squares(h_base, e_base, at):
                for c in range(CT):
                    act.wait_ge(h_written, h_base + at + c + 1)
                    act.wait_ge(sumsq_done, e_base + at + c - (CT - 1))
                    act.activation(gbuf[:, c, :], h[:, at + c, :], ACT.Square).then_inc(squared, 1)

            def down(c_base, m_base, h_base, e_base, gain, n_ks, final=False):
                for group in range(OUT_GROUPS):
                    end = n_ks * (group + 1)
                    at = CT * group
                    last = final and group == OUT_GROUPS - 1
                    splits(c_base, 4 if group == 0 else end - n_ks + 3, end + (0 if last else 2))
                    copy_halves(c_base + end - 1, m_base + at, CT * (group % 2))
                    if not last:
                        splits(c_base, end + 2, end + 3)
                    if gain is not None:
                        for c in range(CT):
                            high(at + c, gain, h_written, h_base + at + c + 1)
                    squares(h_base, e_base, at)
                if not final:
                    splits(c_base, OUT_GROUPS * n_ks + 3, OUT_GROUPS * n_ks + 4)

            def deviation(n, dims):
                act.wait_ge(stat_ready, n + 1)
                act.activation(std[:, :], stat[:, :], ACT.Sqrt, bias=eps[:, 0:1], scale=1.0 / dims
                               ).then_inc(std_ready, 1)

            def mixed_squares(part):
                for t in range(LT):
                    act.wait_ge(sumsq_done, E_LRU + LT * part + t - (CT - 1))
                    act.activation(gbuf[:, t % CT, :], proj[:, (X0, Q0)[part] + t, :], ACT.Square
                                   ).then_inc(squared, 1)

            def mixed_high(part, t0, t1):
                for t in range(t0, t1):
                    act.wait_ge(normed_full, LT * part + t + 1)
                    act.copy(mix_t[:, part, 0, t, :], ubuf[:, t % CT, :]).then_inc(normed_hi, 1)

            act.wait_ge(vec_clear, 2)
            for part in vec_parts[0] + vec_parts[1][:1]:
                load_vector(act, part, vec_landed)
            act.wait_ge(chain, 1)
            act.activation(std[:, 0:1], eps[:, :], ACT.Copy).then_inc(table_in, 1)
            act.wait_ge(vecs_ready, 1)
            for t in range(DT):
                high(t, G_FFN1, bank_free, t // 2 + 1)
                if t % CT == CT - 1 and t < 2 * CT:
                    splits(0, t // CT, t // CT + 1, fill=True)
            splits(0, 2, 3)
            for q in range(DT // CT):
                if q == 3:
                    act.wait_ge(squares_added, 1)
                act.activation(first_squares[q], h4(q), ACT.Square).then_inc(squared, CT)
            splits(0, 3, 6)
            deviation(N_FFN1, D)
            hidden(C_UP1, M_UP1, 0, 0, j0=6)
            with act.Fori(1, UP_BLOCKS) as i:
                hidden(C_UP1, M_UP1, 0, i)
            down(C_DOWN1, M_DOWN1, H_DOWN1, E_DOWN1, G_MIX, DOWN_KS)
            deviation(N_MIX, D)

            def copy_group(s):
                group = mix_chunk(s)[0]
                copy_halves(C_MIX_IN + s, M_MIX_IN + CT * group, first_bank(group))

            def step(s):
                if s > 3 and ends_group(s - 1):
                    copy_group(s - 1)
                splits(C_MIX_IN, s + 1, s + 2)

            def centre(u):
                for t in range(UT * u, UT * (u + 1)):
                    act.wait_ge(proj_scaled, X0 + t + 1)
                    act.activation(proj[:, XC0 + t, :], proj[:, X0 + t, :], ACT.Identity, bias=vec(CONV_B + t),
                                   scale=vec(CONV_W + (CONV_WIDTH // 2) * LT + t)).then_inc(centre_done, 1)

            def sigmoids(t):
                u, c = divmod(t, UT)
                act.wait_ge(gates_ready, t + 1)
                if u >= 2:
                    act.wait_ge(summed, u - 1)
                for z in range(2):
                    for g, dest in enumerate((lru_r[u % 2], lru_i[u % 2])):
                        act.activation(dest[:, c, z, :], psum[:, CT + 2 * c + z, g * T:(g + 1) * T], ACT.Sigmoid,
                                       bias=vec(GATE_B + (2 * z + g) * LT + t)).then_inc(gates_read, 1)

            def tanhs(u):
                act.wait_ge(gates_read, 4 * UT * (u + 1))
                if u == 0:
                    act.wait_ge(decay_ready, 1)
                for c in range(UT):
                    for z in range(2):
                        col = z * LT + UT * u + c
                        act.activation(lru_t[u % 2][:, c, z, :], lru_r[u % 2][:, c, z, :], ACT.Tanh,
                                       scale=decay4[:, col:col + 1]).then_inc(tanh_done, 1)

            def exps(u):
                act.wait_ge(tanh_done, 2 * UT * (u + 1))
                for c in range(UT):
                    for z in range(2):
                        col = z * LT + UT * u + c
                        act.activation(lru_r[u % 2][:, c, z, :], lru_r[u % 2][:, c, z, :], ACT.Exp,
                                       scale=decay8n[:, col:col + 1]).then_inc(decay_done, 1)

            def roots(u):
                act.activation(flat(lru_s[u % 2]), flat(lru_t[u % 2]), ACT.Sqrt).then_inc(sqrt_done, 1)

            def complements(u):
                act.wait_ge(scaled_one, u + 1)
                act.activation(flat(lru_r[u % 2]), flat(lru_t[u % 2]), ACT.Copy, bias=1.0, scale=-1.0
                               ).then_inc(complement_done, 1)

            def gelu_square(hh):
                act.wait_ge(sumsq_done, E_DOWN1 + DT)
                act.wait_ge(proj_scaled, G0 + HLT * (hh + 1))
                act.activation(gelu_tmp[hh], g_half(hh), ACT.Square, scale=0.044715 ** 0.5).then_inc(gelu_sq, 1)

            def gelu_sigmoid(hh):
                act.wait_ge(gelu_arg, hh + 1)
                act.activation(gelu_tmp[hh], gelu_tmp[hh], ACT.Sigmoid, scale=2.0 * (2.0 / math.pi) ** 0.5
                               ).then_inc(gelu_sig, 1)

            def softmax_exps(j, slot0, slot1):
                act.wait_ge(centred, j + 1)
                for slot in range(slot0, slot1):
                    act.activation(prob[:, j, slot, :], prob[:, j, slot, :], ACT.Exp, bias=mx[:, slot:slot + 1],
                                   accum_out=den[:, slot:slot + 1]).then_inc(exp_done, 1)

            def copy_probs(j, pair0, pair1):
                if pair0 == 0:
                    act.wait_ge(att_ready, AT * j)
                for pair in range(pair0, pair1):
                    act.wait_ge(prob_turned, NB * j + pair + 1)
                    act.copy(p_t[:, 2 * pair:2 * pair + 2, :, :].rearrange("p h m q -> p (h m q)"),
                             psum[0:KR2, CT + pair % CT, :]).then_inc(prob_t_ready, 1)

            def copy_attended(j):
                for t in range(AT):
                    act.wait_ge(att_ready, AT * j + 4 * (t // 4 + 1))
                    act.copy(grid(proj[:, Q0 + t, :])[:, :, reversed_columns(j)],
                             psum[:, CT + t // 4, (t % 4) * P:(t % 4 + 1) * P].rearrange("p (r c) -> p r c", c=QC)
                             ).then_inc(att_read, 1)

            step(3)
            act.activation(lam_exp[:, :], vecs[:, LAMBDA:LAMBDA + 2 * LT], ACT.Abs).then_inc(lam_exp_done, 1)
            act.wait_ge(lam_exp_done, 1)
            act.activation(lam_exp[:, :], lam_exp[:, :], ACT.Exp, scale=-1.0).then_inc(lam_exp_done, 1)
            step(4)
            centre(0)
            centre(1)
            step(5)
            sigmoids(0)
            step(6)
            sigmoids(1)
            step(7)
            tanhs(0)
            step(8)
            exps(0)
            centre(2)
            centre(3)
            step(9)
            roots(0)
            step(10)
            sigmoids(2)
            step(11)
            complements(0)
            sigmoids(3)
            step(12)
            tanhs(1)
            gelu_square(0)
            step(13)
            exps(1)
            step(14)
            roots(1)
            step(15)
            sigmoids(4)
            step(16)
            sigmoids(5)
            step(17)
            complements(1)
            tanhs(2)
            gelu_sigmoid(0)
            step(18)
            exps(2)
            gelu_square(1)
            step(19)
            roots(2)
            step(20)
            sigmoids(6)
            step(21)
            sigmoids(7)
            complements(2)
            step(22)
            tanhs(3)
            gelu_sigmoid(1)
            step(23)
            exps(3)
            step(24)
            roots(3)
            step(25)
            step(26)
            complements(3)
            for s in range(27, 30):
                step(s)
            act.wait_ge(lru_done, 1)
            mixed_squares(0)
            step(30)
            deviation(N_LRU, L)
            for s in range(31, 35):
                step(s)
            softmax_exps(0, 0, NH // 2)
            mixed_high(0, 0, CT)
            step(35)
            step(36)
            softmax_exps(0, NH // 2, NH)
            for s in range(37, 41):
                step(s)
            mixed_high(0, CT, LT)
            copy_probs(0, 0, 4)
            softmax_exps(1, 0, NH // 4)
            step(41)
            copy_probs(0, 4, 8)
            step(42)
            softmax_exps(1, NH // 4, 3 * NH // 4)
            step(43)
            softmax_exps(1, 3 * NH // 4, NH)
            step(44)
            copy_attended(0)
            step(45)
            copy_probs(1, 0, 4)
            step(46)
            copy_probs(1, 4, 8)
            step(47)
            copy_attended(1)
            act.wait_ge(att_read, NJ * AT)
            mixed_squares(1)
            copy_group(47)
            deviation(N_ATT, A)
            mixed_high(1, 0, CT)
            splits(C_MIX_IN, 49, 50)
            mixed_high(1, CT, AT)

            for s in range(49, S_END + 3):
                step(s)
                if ends_group(s - 1):
                    at = CT * (mix_chunk(s - 1)[0] - MIX_GROUPS - OUT_GROUPS)
                    for c in range(CT):
                        high(at + c, G_FFN2, h_written, H_ATT + at + c + 1)
                    squares(H_ATT, E_MIX, at)
            deviation(N_FFN2, D)
            with act.Fori(0, UP_BLOCKS) as i:
                hidden(C_UP2, M_UP2, FT, i)
            down(C_DOWN2, M_DOWN2, H_DOWN2, E_DOWN2, None, DOWN_KS, final=True)
            act.wait_ge(stat_ready, N_FINAL + 1)
            act.activation(std[:, 0:2], psum[:, NB - 1, 0:2], ACT.Sqrt, bias=eps[:, 0:1], scale=1.0 / D
                           ).then_inc(std_ready, 1)
            act.wait_ge(rstd_ready, N_FINAL + 1)
            for half in range(2):
                for g in (1, 3):
                    act.wait_ge(fin_turned, 4 * half + g + 1)
                    act.activation(fin_nat[:, half, 512 * g:512 * (g + 1)], psum[:, 4 * half + g, :], ACT.Copy,
                                   scale=rstd[:, half:half + 1]).then_inc(fin_odd, 1)

        @block.vector
        def _(dve):
            linked = [0]

            def link(ins):
                linked[0] += 1
                ins.then_inc(chain, 1)
                dve.wait_ge(chain, linked[0])

            def splits(n0, j0, j1, fill=False):
                for j in range(j0, j1):
                    dve.wait_ge(hi_split, n0 + j + 1)
                    dve.tensor_tensor(w_lo[j % RING][:, :, :], w_raw[j % RING][:, :, :],
                                      w_hi[j % 2][:, :, :].bitcast(F32), ALU.subtract).then_inc(lo_split, 1)

            def add_halves(m, b0, dest):
                for c in range(CT):
                    dve.wait_ge(half_copied, m + c + 1 - NB)
                    dve.tensor_tensor(dest[c], psum[:, b0 + c, 0:T], half_b[:, c, :], ALU.add
                                      ).then_inc(bank_free, 1)

            g_tiles4 = [gbuf[:, c, :] for c in range(CT)]
            u_tiles4 = [ubuf[:, c, :] for c in range(CT)]

            def hidden(c_base, m_base, f_base, i, j0=4):
                n0 = c_base + 2 * UP_KS * i
                m = m_base + 2 * CT * i
                f = f_base + CT * i
                splits(n0, j0, 8)
                add_halves(m, 0, g_tiles4)
                splits(n0, 8, 9)
                add_halves(m + CT, CT, u_tiles4)
                for c in range(CT):
                    dve.wait_ge(bank_free, m + c + 1)
                    dve.tensor_tensor(gbuf[:, c, :], gbuf[:, c, :], rstd[:, :], ALU.mult).then_inc(gate_scaled, 1)
                splits(n0, 9, 10)
                for c in range(CT):
                    dve.wait_ge(bank_free, m + CT + c + 1)
                    dve.tensor_tensor(ubuf[:, c, :], ubuf[:, c, :], rstd[:, :], ALU.mult).then_inc(up_scaled, 1)
                for c in range(CT):
                    dve.wait_ge(silu_done, f + c + 1)
                    dve.wait_ge(up_scaled, f + c + 1)
                    dve.tensor_tensor(ubuf[:, c, :], gbuf[:, c, :], ubuf[:, c, :], ALU.mult
                                      ).then_inc(hidden_full, 1)
                splits(n0, 10, 11)
                for c in range(CT):
                    dve.wait_ge(hidden_hi, f + c + 1)
                    dve.tensor_tensor(hid_t[:, CT * i + c, 1, :], ubuf[:, c, :],
                                      hid_t[:, CT * i + c, 0, :].bitcast(F32), ALU.subtract
                                      ).then_inc(hidden_ready, 1)
                splits(n0, 11, 12)

            def sum_squares(e, first=False):
                for c in range(CT):
                    dve.wait_ge(squared, e + c + 1)
                    if not (first and c == 0):
                        dve.wait_ge(sumsq_done, e + c)
                    dve.tensor_tensor(sumsq[:, :], sumsq[:, :], gbuf[:, c, :], ALU.add).then_inc(sumsq_done, 1)

            def low(count, t, gain):
                dve.wait_ge(act_hi, count)
                dve.scalar_tensor_tensor(act_t[:, t, 1, :], h[:, t, :], vec(gain + t),
                                         act_t[:, t, 0, :].bitcast(F32), ALU.mult, ALU.subtract
                                         ).then_inc(act_ready, 1)

            def down(c_base, m_base, h_base, e_base, hi_base, gain, n_ks, scale, final=False):
                for group in range(OUT_GROUPS):
                    end = n_ks * (group + 1)
                    at = CT * group
                    last = final and group == OUT_GROUPS - 1
                    splits(c_base, 4 if group == 0 else end - n_ks + 3, end + (0 if last else 2))
                    add_halves(m_base + at, CT * (group % 2), u_tiles4)
                    for c in range(CT):
                        dve.wait_ge(bank_free, m_base + at + c + 1)
                        dve.scalar_tensor_tensor(h[:, at + c, :], ubuf[:, c, :], scale, h[:, at + c, :],
                                                 ALU.mult, ALU.add).then_inc(h_written, 1)
                    if not last:
                        splits(c_base, end + 2, end + 3)
                    for c in range(CT):
                        if gain is None:
                            dve.wait_ge(h_written, h_base + at + c + 1)
                            dve.tensor_scalar(fin_t[:, at + c, :], h[:, at + c, :], vec(G_FINAL + at + c), None,
                                              ALU.mult).then_inc(fin_scaled, 1)
                        else:
                            low(hi_base + at + c + 1, at + c, gain)
                    if not last:
                        sum_squares(e_base + at)
                if not final:
                    splits(c_base, OUT_GROUPS * n_ks + 3, OUT_GROUPS * n_ks + 4)

            def scales(n, dest=rstd):
                dve.wait_ge(stat_ready, n + 1)
                dve.memset(sumsq[:, :], 0.0).then_inc(sumsq_clear, 1)
                dve.wait_ge(std_ready, n + 1)
                dve.reciprocal(dest[:, :], std[:, :]).then_inc(rstd_ready, 1)
                dve.wait_ge(rstd_ready, n + 1)
                dve.wait_ge(sumsq_clear, n + 1)

            def normalise(part, t0, t1):
                def low_mix(t):
                    dve.wait_ge(normed_hi, LT * part + t + 1)
                    dve.tensor_tensor(mix_t[:, part, 1, t, :], ubuf[:, t % CT, :],
                                      mix_t[:, part, 0, t, :].bitcast(F32), ALU.subtract).then_inc(act_ready, 1)

                for t in range(t0, t1):
                    dve.scalar_tensor_tensor(ubuf[:, t % CT, :], proj[:, (X0, Q0)[part] + t, :],
                                             vec((G_LRU, G_ATT)[part] + t), mix_rstd[:, :],
                                             ALU.mult, ALU.mult).then_inc(normed_full, 1)
                    if t > t0:
                        low_mix(t - 1)
                low_mix(t1 - 1)

            for s in range(2):
                dve.memset(vec_rows[s][:, :], 0.0).then_inc(vec_clear, 1)
            link(dve.memset(eps[:, :], EPS))
            for b in range(NB):
                if b == NB - 1:
                    dve.wait_ge(vec_turned, 1)
                    dve.tensor_copy(vecs[:, :], psum[:, b, 0:2 * P]).then_inc(vecs_ready, 1)
                dve.wait_ge(x_turned, b + 1)
                dve.tensor_copy(h[:, 2 * b:2 * b + 2, :].rearrange("p a t -> p (a t)"), psum[:, b, :]
                                ).then_inc(bank_free, 1)
            dve.wait_ge(vecs_ready, 1)
            dve.wait_ge(bank_free, NB)
            for t in range(DT):
                low(t + 1, t, G_FFN1)
                if t % CT == CT - 1 and t < 2 * CT:
                    splits(0, t // CT, t // CT + 1)
            splits(0, 2, 3)
            dve.wait_ge(squared, CT)
            for q in range(1, DT // CT):
                dve.wait_ge(squared, CT * (q + 1))
                if q > 1:
                    dve.wait_ge(squares_added, q - 1)
                dve.tensor_tensor(first_squares[0], first_squares[0], first_squares[q], ALU.add
                                  ).then_inc(squares_added, 1)
            dve.wait_ge(squares_added, DT // CT - 1)
            half = CT // 2 * T
            link(dve.tensor_tensor(first_squares[0][:, 0:half], first_squares[0][:, 0:half],
                                   first_squares[0][:, half:2 * half], ALU.add))
            dve.tensor_tensor(sumsq[:, :], gbuf[:, 0, :], gbuf[:, 1, :], ALU.add).then_inc(sumsq_done, DT)
            splits(0, 3, 6)
            scales(N_FFN1)
            hidden(C_UP1, M_UP1, 0, 0, j0=6)
            with dve.Fori(1, UP_BLOCKS) as i:
                hidden(C_UP1, M_UP1, 0, i)
            down(C_DOWN1, M_DOWN1, H_DOWN1, E_DOWN1, DT, G_MIX, DOWN_KS, 0.5)
            scales(N_MIX)

            def evacuate(s):
                group = mix_chunk(s)[0]
                m = M_MIX_IN + CT * group
                if s < S_OUT:
                    tiles = [proj[:, CT * group + c, :] for c in range(CT)]
                    add_halves(m, first_bank(group), tiles)
                    for c in range(CT):
                        dve.wait_ge(bank_free, m + c + 1)
                        dve.tensor_tensor(tiles[c], tiles[c], rstd[:, :], ALU.mult).then_inc(proj_scaled, 1)
                else:
                    at = CT * (group - MIX_GROUPS)
                    add_halves(m, first_bank(group), u_tiles4)
                    for c in range(CT):
                        dve.wait_ge(bank_free, m + c + 1)
                        dve.wait_ge(h_written, H_LRU + max(0, at + c - DT + 1))
                        dve.tensor_tensor(h[:, (at + c) % DT, :], h[:, (at + c) % DT, :], ubuf[:, c, :], ALU.add
                                          ).then_inc(h_written, 1)

            def step(s):
                splits(C_MIX_IN, s + 1, s + 2)
                if ends_group(s):
                    evacuate(s)

            def decay_rates():
                dve.wait_ge(lam_exp_done, 2)
                link(dve.tensor_scalar(sp_s2[:, :], lam_exp[:, :], 2.0, None, ALU.add))
                link(dve.reciprocal(sp_s[:, :], sp_s2[:, :]))
                link(dve.tensor_tensor(sp_s[:, :], sp_s[:, :], lam_exp[:, :], ALU.mult))
                link(dve.tensor_tensor(sp_s2[:, :], sp_s[:, :], sp_s[:, :], ALU.mult))
                link(dve.tensor_scalar(sp_q[:, :], sp_s2[:, :], 1.0 / 17, None, ALU.mult))
                for k in range(7, 0, -1):
                    link(dve.scalar_tensor_tensor(sp_q[:, :], sp_q[:, :], 1.0 / (2 * k + 1), sp_s2[:, :],
                                                  ALU.add, ALU.mult))
                link(dve.scalar_tensor_tensor(sp_q[:, :], sp_q[:, :], 1.0, sp_s[:, :], ALU.add, ALU.mult))
                link(dve.tensor_scalar(sp_s[:, :], vecs[:, LAMBDA:LAMBDA + 2 * LT], -1.0, 0.0, ALU.mult, ALU.max))
                link(dve.scalar_tensor_tensor(sp_s[:, :], sp_q[:, :], 2.0, sp_s[:, :], ALU.mult, ALU.add))
                link(dve.tensor_scalar(decay4[:, :], sp_s[:, :], RG_C / 2, None, ALU.mult))
                dve.tensor_scalar(decay8n[:, :], sp_s[:, :], -RG_C, None, ALU.mult).then_inc(decay_ready, 1)

            def convolve(u):
                for t in range(UT * u, UT * (u + 1)):
                    xin, xc = proj[:, X0 + t, :], proj[:, XC0 + t, :]
                    centre = CONV_WIDTH // 2
                    dve.wait_ge(centre_done, t + 1)
                    for w in (0, 1, 3):
                        d = w - centre
                        o0, o1 = max(0, -d), T - max(0, d)
                        tap = dve.scalar_tensor_tensor(xc[:, o0:o1], xin[:, o0 + d:o1 + d],
                                                       vec(CONV_W + w * LT + t), xc[:, o0:o1], ALU.mult, ALU.add)
                        if w < 3:
                            link(tap)
                        else:
                            tap.then_inc(conv_done, 1)

            def gated_input(u):
                dve.wait_ge(conv_done, UT * (u + 1))
                dve.wait_ge(gates_read, 4 * UT * (u + 1))
                i = lru_i[u % 2]
                for z in range(2):
                    link(dve.tensor_tensor(i[:, :, z, :], i[:, :, z, :], proj[:, XC0 + UT * u:XC0 + UT * (u + 1), :],
                                           ALU.mult))

            def decays(u):
                r, t, root = flat(lru_r[u % 2]), flat(lru_t[u % 2]), flat(lru_s[u % 2])
                dve.wait_ge(decay_done, 2 * UT * (u + 1))
                dve.wait_ge(sqrt_done, u + 1)
                link(dve.scalar_tensor_tensor(root, r, 1.0, root, ALU.add, ALU.mult))
                dve.scalar_tensor_tensor(t, r, 1.0, t, ALU.add, ALU.mult).then_inc(scaled_one, 1)
                link(dve.tensor_tensor(flat(lru_i[u % 2]), root, flat(lru_i[u % 2]), ALU.mult))

            def scan(u):
                r, i, out = lru_r[u % 2], lru_i[u % 2], lru_s[u % 2]
                dve.wait_ge(complement_done, u + 1)
                for c in range(UT):
                    dve.tensor_tensor_scan(out[:, c, 0, :], r[:, c, 0, :], i[:, c, 0, :], 0.0,
                                           ALU.mult, ALU.add).then_inc(scanned, 1)
                    dve.tensor_tensor_scan(out[:, c, 1, ::-1], r[:, c, 1, ::-1], i[:, c, 1, ::-1], 0.0,
                                           ALU.mult, ALU.add).then_inc(scanned, 1)
                dve.wait_ge(scanned, 2 * UT * (u + 1))
                dve.tensor_tensor(proj[:, X0 + UT * u:X0 + UT * (u + 1), :], out[:, :, 0, :], out[:, :, 1, :],
                                  ALU.add).then_inc(summed, 1)

            def gelu_argument(hh):
                dve.wait_ge(gelu_sq, hh + 1)
                dve.scalar_tensor_tensor(gelu_tmp[hh], gelu_tmp[hh], 1.0, g_half(hh), ALU.add, ALU.mult
                                         ).then_inc(gelu_arg, 1)

            def gelu(hh):
                dve.wait_ge(gelu_sig, hh + 1)
                dve.tensor_tensor(g_half(hh), g_half(hh), gelu_tmp[hh], ALU.mult).then_inc(gelu_done, 1)

            def softmax_scores(n0, n1):
                for n in range(n0, n1):
                    j, g = divmod(n, len(SCORE_BANKS))
                    s0, s1 = SCORE_BANKS[g]
                    dve.wait_ge(bias_ready, j + 1)
                    dve.wait_ge(scores_ready, n + 1)
                    dve.scalar_tensor_tensor(prob[:, j, s0:s1, :].rearrange("p h k -> p (h k)"),
                                             psum[:, CT + n % CT, 0:(s1 - s0) * NK], HD ** -0.5,
                                             bias[:, j, s0:s1, :].rearrange("p h k -> p (h k)"),
                                             ALU.mult, ALU.add).then_inc(scores_read, 1)

            def softmax_max(j):
                dve.wait_ge(scores_read, len(SCORE_BANKS) * (j + 1))
                link(dve.tensor_reduce(mx[:, :], prob[:, j, :, :], AX_X, ALU.max))
                dve.tensor_scalar(mx[:, :], mx[:, :], -1.0, None, ALU.mult).then_inc(centred, 1)

            def softmax_scale(j):
                dve.wait_ge(exp_done, NH * (j + 1))
                link(dve.reciprocal(rden[:, :], den[:, :]))
                dve.tensor_tensor(prob[:, j, :, :], prob[:, j, :, :],
                                  rden[:, :].unsqueeze(2).broadcast_to([P, NH, NK]), ALU.mult
                                  ).then_inc(prob_ready, 1)

            def gather_values():
                dve.wait_ge(scores_read, NJ * len(SCORE_BANKS))
                dve.wait_ge(proj_scaled, V0 + AT)
                v_rows = proj[:, V0:V0 + AT, :].rearrange("p t (r c) -> p t r c", c=GRID_W)
                for j in range(NJ):
                    for m in range(2):
                        dve.tensor_copy(v_keys[:, j, m, :, :].rearrange("p t (r c) -> p t r c", c=KC),
                                        v_rows[:, :, 2 * m:2 * m + 2, j * KS0:j * KS0 + KC]
                                        ).then_inc(keys_gathered, 1)

            def copy_values(g0, g1):
                for g in range(g0, g1):
                    dve.wait_ge(v_turned, g + 1)
                    dve.tensor_copy(v_nat[:, g // 4, (g // 2) % 2, (g % 2) * 512:(g % 2 + 1) * 512],
                                    psum[0:KR2, CT + g % CT, :]).then_inc(v_ready, 1)

            step(3)
            step(4)
            convolve(0)
            step(5)
            convolve(1)
            step(6)
            decay_rates()
            step(7)
            step(8)
            gated_input(0)
            step(9)
            convolve(2)
            step(10)
            decays(0)
            step(11)
            step(12)
            gelu_argument(0)
            step(13)
            scan(0)
            gated_input(1)
            step(14)
            convolve(3)
            step(15)
            step(16)
            decays(1)
            step(17)
            scan(1)
            step(18)
            gated_input(2)
            step(19)
            step(20)
            decays(2)
            gelu_argument(1)
            step(21)
            gelu(0)
            step(22)
            scan(2)
            step(23)
            step(24)
            gated_input(3)
            gelu(1)
            step(25)
            decays(3)
            step(26)
            scan(3)
            step(27)
            step(28)
            dve.wait_ge(summed, UNITS)
            dve.wait_ge(gelu_done, 2)
            dve.tensor_tensor(proj[:, X0:X0 + LT, :], proj[:, X0:X0 + LT, :], proj[:, G0:G0 + LT, :], ALU.mult
                              ).then_inc(lru_done, 1)
            step(29)
            for t in range(0, LT, CT):
                sum_squares(E_LRU + t)
            step(30)
            scales(N_LRU, mix_rstd)
            step(31)
            step(32)
            softmax_scores(0, 4)
            step(33)
            softmax_scores(4, 6)
            softmax_max(0)
            step(34)
            normalise(0, 0, CT)
            step(35)
            step(36)
            softmax_scores(6, 10)
            step(37)
            softmax_scale(0)
            step(38)
            softmax_scores(10, 12)
            softmax_max(1)
            step(39)
            step(40)
            normalise(0, CT, LT)
            gather_values()
            step(41)
            step(42)
            copy_values(0, 4)
            splits(C_MIX_IN, 44, 45)
            copy_values(4, 8)
            evacuate(43)
            step(44)
            softmax_scale(1)
            step(45)
            step(46)
            splits(C_MIX_IN, 48, 49)
            for t in range(0, AT, CT):
                sum_squares(E_ATT + t)
            evacuate(47)
            scales(N_ATT, mix_rstd)
            normalise(1, 0, CT)
            step(48)
            normalise(1, CT, AT)

            for s in range(49, S_END + 3):
                step(s)
                if ends_group(s - 1):
                    at = CT * (mix_chunk(s - 1)[0] - MIX_GROUPS - OUT_GROUPS)
                    for c in range(CT):
                        low(2 * DT + at + c + 1, at + c, G_FFN2)
                    sum_squares(E_MIX + at)
            scales(N_FFN2)
            with dve.Fori(0, UP_BLOCKS) as i:
                hidden(C_UP2, M_UP2, FT, i)
            down(C_DOWN2, M_DOWN2, H_DOWN2, E_DOWN2, 0, None, DOWN_KS, 0.5, final=True)
            dve.wait_ge(std_ready, N_FINAL + 1)
            dve.reciprocal(rstd[:, 0:2], std[:, 0:2]).then_inc(rstd_ready, 1)
            dve.wait_ge(rstd_ready, N_FINAL + 1)
            for half in range(2):
                for g in (0, 2):
                    dve.wait_ge(fin_turned, 4 * half + g + 1)
                    dve.tensor_scalar(fin_nat[:, half, 512 * g:512 * (g + 1)], psum[:, 4 * half + g, :],
                                      rstd[:, half:half + 1], None, ALU.mult).then_inc(fin_even, 1)


_INS = ['x', 'norm_ffn1', 'ffn1_w_in', 'ffn1_w_out', 'norm_mix', 'w_in_mix', 'lru_conv_w', 'lru_conv_b',
        'lru_gate_w', 'lru_gate_b', 'lru_lambda', 'attn_rpb', 'lru_out_norm', 'attn_out_norm', 'w_out_mix',
        'norm_ffn2', 'ffn2_w_in', 'ffn2_w_out', 'norm_final']
_OUTS = [((1, 256, 2048), 'float32')]


def kernel(**inputs):
    import numpy as _np
    import concourse.bacc as _bacc
    from concourse import mybir as _mybir
    from concourse.bass_utils import run_bass_kernel_spmd as _run

    nc = _bacc.Bacc("TRN2", target_bir_lowering=False, num_devices=1)
    arrays, args = {}, []
    for name in _INS:
        a = _np.ascontiguousarray(inputs[name])
        arrays[f"in_{name}_dram"] = a
        args.append(nc.dram_tensor(f"in_{name}_dram", a.shape, _mybir.dt.from_np(a.dtype), kind="ExternalInput").ap())
    for i, (shape, dtype) in enumerate(_OUTS):
        dt = _mybir.dt.from_np(_np.dtype(dtype))
        args.append(nc.dram_tensor(f"out_{i}_dram", shape, dt, kind="ExternalOutput").ap())
    hybrid_encoder_block(nc, *args)
    r = _run(nc, [arrays], core_ids=[0])
    got = tuple(r.results[0][f"out_{i}_dram"] for i in range(len(_OUTS)))
    return got[0]
```
